# Optimizing a Trainium2 kernel written in Bass

```python
import jax, jax.numpy as jnp
from jax import lax
import numpy as np

D_MODEL = 1024
BATCH = 1
SEQ = 256
DEPTH = 2

CTX_LEN = 256
GRID_W = 64
HG_HEADS = 4
HG_DK = 128
HG_DV = 128
HG_WIDTH = HG_HEADS * HG_DK
POOL_WINDOWS = (2, 4, 8, 16)
POOL_GROUPS = len(POOL_WINDOWS)
POOL_WIDTH = 512
POOL_GD = POOL_WIDTH // POOL_GROUPS
D_FF = 2816
CHUNK = 64
N_MOD = 9
EPS = 1e-6
IN_SIZES = (HG_WIDTH, HG_WIDTH, HG_WIDTH, HG_HEADS * HG_DV, HG_HEADS * HG_DV, POOL_WIDTH, D_MODEL, D_MODEL)
IN_COLS = sum(IN_SIZES)
IN_SPLITS = tuple(int(s) for s in np.cumsum(IN_SIZES)[:-1])

kernel_name = 'hgrn2_pool_macaron_hybrid'

def rmsnorm(x, w):
    xf = x.astype(jnp.float32)
    y = xf * lax.rsqrt(jnp.mean(xf * xf, axis=-1, keepdims=True) + EPS)
    return (y * w.astype(jnp.float32)).astype(x.dtype)

def modulate(x, shift, scale):
    return x * (1 + scale) + shift

def ffn_half(h, mod, k0, norm_w, wg, wu, wd):
    u = modulate(rmsnorm(h, norm_w), mod[:, k0, None], mod[:, k0 + 1, None])
    y = (jax.nn.silu(u @ wg) * (u @ wu)) @ wd
    return h + 0.5 * mod[:, k0 + 2, None] * y

def gla_scan(q, k, v, log_f, s0):
    b, n, h, _ = q.shape
    nc = n // CHUNK

    def to_chunks(t):
        return jnp.moveaxis(t.astype(jnp.float32).reshape(b, nc, CHUNK, h, t.shape[-1]), 1, 0)

    mask = jnp.tril(jnp.ones((CHUNK, CHUNK), dtype=bool))

    def step(state, inp):
        qc, kc, vc, lf = inp
        cum = jnp.cumsum(lf, axis=1)
        inter = jnp.einsum('bchd,bhde->bche', qc * jnp.exp(cum), state)
        diff = cum[:, :, None] - cum[:, None]
        decay = jnp.exp(jnp.where(mask[None, :, :, None, None], diff, -jnp.inf))
        attn = jnp.einsum('btshd,bshd->bhts', qc[:, :, None] * decay, kc)
        intra = jnp.einsum('bhts,bshe->bthe', attn, vc)
        last = cum[:, -1]
        k_dec = kc * jnp.exp(last[:, None] - cum)
        new_state = jnp.exp(last)[..., None] * state + jnp.einsum('bshd,bshe->bhde', k_dec, vc)
        return new_state, inter + intra

    s_fin, out = lax.scan(step, s0, (to_chunks(q), to_chunks(k), to_chunks(v), to_chunks(log_f)))
    out = jnp.moveaxis(out, 0, 1).reshape(b, n, h, v.shape[-1])
    return out, s_fin

def hgrn2_bidir(q, i, zf, zb, lb_f, lb_b, s0_f, s0_b):
    b, n, _ = q.shape

    def heads(t):
        return t.astype(jnp.float32).reshape(b, n, HG_HEADS, -1)

    qh = jax.nn.silu(heads(q))
    vh = heads(i)

    def gates(z, lb):
        z = heads(z)
        lb = lb.astype(jnp.float32).reshape(HG_HEADS, HG_DK)
        f = lb + (1 - lb) * jax.nn.sigmoid(z)
        return (1 - lb) * jax.nn.sigmoid(-z), jnp.log(f)

    kf, lff = gates(zf, lb_f)
    kb, lfb = gates(zb, lb_b)
    o_f, s_f = gla_scan(qh, kf, vh, lff, s0_f)
    flip = lambda t: jnp.flip(t, axis=1)
    o_b, s_b = gla_scan(flip(qh), flip(kb), flip(vh), flip(lfb), s0_b)
    return o_f + flip(o_b), s_f, s_b

def box_mean(x, axis, w):
    length = x.shape[axis]
    cs = jnp.cumsum(x, axis=axis)
    cs = jnp.concatenate([jnp.zeros_like(lax.slice_in_dim(cs, 0, 1, axis=axis)), cs], axis=axis)
    idx = jnp.arange(length)
    lo = jnp.clip(idx - w // 2, 0, length)
    hi = jnp.clip(idx + w - w // 2, 0, length)
    s = jnp.take(cs, hi, axis=axis) - jnp.take(cs, lo, axis=axis)
    shape = [1] * x.ndim
    shape[axis] = length
    return s / (hi - lo).astype(jnp.float32).reshape(shape)

def pool_mixer(v, pool_w, pool_scale, on_grid):
    b, n, _ = v.shape
    vf = v.astype(jnp.float32)
    if on_grid:
        rows = n // GRID_W
        vf = vf.reshape(b, rows, GRID_W, POOL_WIDTH)
    outs = []
    for gi, w in enumerate(POOL_WINDOWS):
        seg = vf[..., gi * POOL_GD:(gi + 1) * POOL_GD]
        m = box_mean(box_mean(seg, 2, w), 1, w) if on_grid else box_mean(seg, 1, w)
        outs.append(m - seg)
    d = jnp.stack(outs, axis=-2).reshape(b, n, POOL_GROUPS, POOL_GD)
    y = jnp.einsum('bngc,gcd->bngd', d, pool_w.astype(jnp.float32)).reshape(b, n, POOL_WIDTH)
    return (y * pool_scale.astype(jnp.float32)).astype(v.dtype)

def mixer(u, w_in, lb_f, lb_b, hg_norm_w, pool_w, pool_scale, w_a, w_b, w_out, s0_f, s0_b, on_grid, need_out):
    proj = u @ w_in
    q, zf, zb, i, g, pv, ga, gb = jnp.split(proj, IN_SPLITS, axis=-1)
    o, s_f, s_b = hgrn2_bidir(q, i, zf, zb, lb_f, lb_b, s0_f, s0_b)
    if not need_out:
        return None, s_f, s_b
    b, n = u.shape[0], u.shape[1]
    on = o * lax.rsqrt(jnp.mean(o * o, axis=-1, keepdims=True) + EPS)
    on = on * hg_norm_w.astype(jnp.float32).reshape(HG_HEADS, HG_DV)
    a = (on.reshape(b, n, HG_HEADS * HG_DV) * jax.nn.silu(g.astype(jnp.float32))).astype(u.dtype)
    p = pool_mixer(pv, pool_w, pool_scale, on_grid)
    merged = jax.nn.sigmoid(ga) * (a @ w_a) + jax.nn.sigmoid(gb) * (p @ w_b)
    return merged @ w_out, s_f, s_b

def setup_inputs(seed: int = 0) -> dict:
    key = jax.random.key(seed)
    ks = jax.random.split(key, 19)
    nrm = lambda k, shape, s: jax.random.normal(k, shape, jnp.float32) * s
    return {
        'x': nrm(ks[0], (BATCH, SEQ, D_MODEL), 1.0),
        'c': nrm(ks[1], (BATCH, D_MODEL), 1.0),
        'ctx': nrm(ks[2], (BATCH, CTX_LEN, D_MODEL), 1.0),
        'c_ctx': nrm(ks[3], (D_MODEL,), 1.0),
        'ada_w': nrm(ks[4], (DEPTH, D_MODEL, N_MOD * D_MODEL), D_MODEL ** -0.5),
        'ada_b': nrm(ks[5], (DEPTH, N_MOD * D_MODEL), 0.02),
        'norm_w': 1.0 + nrm(ks[6], (DEPTH, 3, D_MODEL), 0.02),
        'ffn_wg': nrm(ks[7], (DEPTH, 2, D_MODEL, D_FF), D_MODEL ** -0.5),
        'ffn_wu': nrm(ks[8], (DEPTH, 2, D_MODEL, D_FF), D_MODEL ** -0.5),
        'ffn_wd': nrm(ks[9], (DEPTH, 2, D_FF, D_MODEL), D_FF ** -0.5),
        'w_in': nrm(ks[10], (DEPTH, D_MODEL, IN_COLS), D_MODEL ** -0.5),
        'lower_bounds': nrm(ks[11], (2, DEPTH, HG_WIDTH), 0.5),
        'hg_norm_w': 1.0 + nrm(ks[12], (DEPTH, HG_HEADS * HG_DV), 0.02),
        'pool_w': nrm(ks[13], (DEPTH, POOL_GROUPS, POOL_GD, POOL_GD), POOL_GD ** -0.5),
        'pool_scale': 1.0 + nrm(ks[14], (DEPTH, POOL_WIDTH), 0.02),
        'w_branch_a': nrm(ks[15], (DEPTH, HG_HEADS * HG_DV, D_MODEL), (HG_HEADS * HG_DV) ** -0.5),
        'w_branch_b': nrm(ks[16], (DEPTH, POOL_WIDTH, D_MODEL), POOL_WIDTH ** -0.5),
        'w_out': nrm(ks[17], (DEPTH, D_MODEL, D_MODEL), D_MODEL ** -0.5),
        'final_norm_w': 1.0 + nrm(ks[18], (D_MODEL,), 0.02),
    }

def reference(x, c, ctx, c_ctx, ada_w, ada_b, norm_w, ffn_wg, ffn_wu, ffn_wd, w_in, lower_bounds,
              hg_norm_w, pool_w, pool_scale, w_branch_a, w_branch_b, w_out, final_norm_w):
    b = x.shape[0]
    h, hc = x, ctx
    silu_c = jax.nn.silu(c)
    silu_cc = jax.nn.silu(c_ctx)[None]
    sm = jax.nn.softmax(lower_bounds.astype(jnp.float32), axis=1)
    lbs = jnp.cumsum(sm, axis=1) - sm[:, :1]
    zeros_state = jnp.zeros((b, HG_HEADS, HG_DK, HG_DV), jnp.float32)
    for l in range(DEPTH):
        last = l == DEPTH - 1
        mod_lat = (silu_c @ ada_w[l] + ada_b[l]).reshape(b, N_MOD, D_MODEL)
        mod_ctx = (silu_cc @ ada_w[l] + ada_b[l]).reshape(1, N_MOD, D_MODEL)
        mix_args = (w_in[l], lbs[0, l], lbs[1, l], hg_norm_w[l], pool_w[l], pool_scale[l],
                    w_branch_a[l], w_branch_b[l], w_out[l])
        h = ffn_half(h, mod_lat, 0, norm_w[l, 0], ffn_wg[l, 0], ffn_wu[l, 0], ffn_wd[l, 0])
        hc = ffn_half(hc, mod_ctx, 0, norm_w[l, 0], ffn_wg[l, 0], ffn_wu[l, 0], ffn_wd[l, 0])
        uc = modulate(rmsnorm(hc, norm_w[l, 1]), mod_ctx[:, 3, None], mod_ctx[:, 4, None])
        y_c, s_f, s_b = mixer(uc, *mix_args, zeros_state, zeros_state, False, not last)
        u = modulate(rmsnorm(h, norm_w[l, 1]), mod_lat[:, 3, None], mod_lat[:, 4, None])
        y, _, _ = mixer(u, *mix_args, s_f, s_b, True, True)
        h = h + mod_lat[:, 5, None] * y
        h = ffn_half(h, mod_lat, 6, norm_w[l, 2], ffn_wg[l, 1], ffn_wu[l, 1], ffn_wd[l, 1])
        if not last:
            hc = hc + mod_ctx[:, 5, None] * y_c
            hc = ffn_half(hc, mod_ctx, 6, norm_w[l, 2], ffn_wg[l, 1], ffn_wu[l, 1], ffn_wd[l, 1])
    return rmsnorm(h, final_norm_w)


_drawn_inputs = setup_inputs


def setup_inputs(seed=0):
    import zlib

    import numpy as np

    out = dict(_drawn_inputs(seed))
    spreads = {}
    factors = {'ctx': 5.795,
     'c_ctx': 4.887,
     'norm_w': 2.801,
     'lower_bounds': 8.0,
     'hg_norm_w': 8.0,
     'pool_scale': 6.244,
     'final_norm_w': 2.903}
    for name, (base, spread) in spreads.items():
        noise = np.random.default_rng([zlib.crc32(name.encode()), seed]).standard_normal(out[name].shape)
        drawn = base * np.exp(spread * noise) if base else spread * noise
        out[name] = __import__('jax').numpy.asarray(drawn.astype(out[name].dtype))
    for name, factor in factors.items():
        out[name] = (out[name] * factor).astype(out[name].dtype)
    return out
```

```python
from contextlib import ExitStack

import numpy as np

import concourse.bass as bass
import concourse.mybir as mybir
from concourse.alu_op_type import AluOpType as ALU

ACT = mybir.ActivationFunctionType
F32 = mybir.dt.float32
F32R = mybir.dt.float32r
BF16 = mybir.dt.bfloat16
U8 = mybir.dt.uint8

P = 128
D = 1024
ND = D // P
TOK = 256
ALL = 2 * TOK
NLAYER = 2
NMOD = 9
NF = 2816 // P
PARTS = (8, 8, 6)
NH = 4
NG = 4
WINDOWS = (2, 4, 8, 16)
GRID_W = 64
EPS = 1e-6
UNIT = 1024
RING = 4
AHEAD = 3
START = 2 * ND
NLEVEL = 7
STEP_CROSS, STEP_STATE = NLEVEL + 1, NLEVEL + 2
NSTEP = NLEVEL + 3

FFN_UNITS = 2 * NF + len(PARTS) * ND
MIX_UNITS = 4 + 4 + 3 * 6 + 6 + 2 * ND + ND
LAYER_UNITS = 2 * FFN_UNITS + MIX_UNITS
N_UNITS = START + NLAYER * LAYER_UNITS
FFN_ADA = FFN_UNITS // 2
N_ADA = NLAYER * NMOD * ND - START

C_NORM = 0
C_ADAB = C_NORM + NLAYER * 3 * ND
C_HGW = C_ADAB + NLAYER * NMOD * ND
C_PSC = C_HGW + NLAYER * NH
C_LB = C_PSC + NLAYER * NG
C_FIN = C_LB + 2 * NLAYER * NH
N_COLS = C_FIN + ND


def ffn_base(layer, which):
    return START + layer * LAYER_UNITS + which * (FFN_UNITS + MIX_UNITS)


def mix_base(layer):
    return START + layer * LAYER_UNITS + FFN_UNITS


def ada_plan():
    plan, at = {}, 0
    for key, n in (((0, "ffn0"), FFN_ADA), ((0, "mix"), 2 * ND), ((0, "ffn1"), FFN_ADA),
                   ((1, "ffn0"), FFN_ADA), ((1, "mix"), ND + 2)):
        plan[key] = (at, n)
        at += n
    assert at == N_ADA
    return plan


ADA = ada_plan()


def program(nc, resid_in, c_in, c_cols_in, cols_in, poolw_in, box_in, masks_in, ident_in, weights, adaw, out):
    with ExitStack() as stack:
        sem = lambda name: stack.enter_context(nc.semaphore(name))

        at = [16640]

        def sb(name, shape, dt=F32, where=None):
            size = int(np.prod(shape[1:])) * mybir.dt.size(dt)
            offset = at[0] if where is None else where
            if where is None:
                at[0] += (size + 31) // 32 * 32
            return nc.alloc_sbuf_tensor_at(name, list(shape), dt, offset=offset), offset

        raw, raw_at = sb("raw", [P, RING, UNIT])
        w_lo, _ = sb("w_lo", [P, RING, ND, P], F32R, raw_at)
        w_hi, _ = sb("w_hi", [P, RING, ND, P], F32R)
        ada_raw, _ = sb("ada_raw", [P, 2, D])
        silu_c, _ = sb("silu_c", [P, 2, D])
        junk, _ = sb("junk", [P, 2, D], BF16)
        u_hi, _ = sb("u_hi", [P, ND, ALL], F32R)
        u_lo, _ = sb("u_lo", [P, ND, ALL], F32R)
        h, _ = sb("h", [P, ND, ALL])
        hid_hi, hid_hi_at = sb("hid_hi", [P, 8, ALL], F32R)
        hid_lo, hid_lo_at = sb("hid_lo", [P, 8, ALL], F32R)
        a_hi, a_lo = hid_hi[:, 0:4, :], hid_lo[:, 0:4, :]
        p_hi, p_lo = hid_hi[:, 4:8, :], hid_lo[:, 4:8, :]
        box = [sb(f"box{s}", [P, 2, NG, TOK], F32, at_)[0]
               for s, at_ in enumerate((hid_hi_at + 8192, hid_lo_at + 8192))]
        S, T, A, AX, scan_at = [], [], [], [], []
        for par in range(2):
            t, where = sb(f"S{par}", [P, 4, ALL])
            scan_at.append(where)
            S.append(t)
            T.append(sb(f"T{par}", [P, 2, ALL])[0])
            A.append(sb(f"A{par}", [P, 2, 2 * TOK])[0])
            AX.append(sb(f"AX{par}", [P, 2, TOK])[0])
        v, _ = sb("v", [P, 4, NH * P])
        gs, _ = sb("gs", [P, 2, ALL])
        sig_a, _ = sb("sig_a", [P, ND, ALL])
        silu_t, _ = sb("silu_t", [P, 2, ALL], F32, scan_at[0])
        hid_t, _ = sb("hid_t", [P, 2, ALL], F32, scan_at[0] + 4096)
        pv, _ = sb("pv", [P, 4, NG * P], F32, scan_at[0])
        dpool, _ = sb("dpool", [P, NG, ALL], F32, scan_at[0] + 8192)
        sq, _ = sb("sq", [P, 2, ALL], F32, scan_at[1])
        sq_sum, _ = sb("sq_sum", [P, ALL], F32, scan_at[1] + 4096)
        diag, _ = sb("diag", [P, ALL // P, P], F32, scan_at[1] + 6144)
        norm_t, _ = sb("norm_t", [P, 4, ALL], F32, scan_at[1] + 8192)
        sig_b, _ = sb("sig_b", [P, 2, ALL], F32, scan_at[1])
        mix_t, _ = sb("mix_t", [P, 2, 2, ALL], F32, scan_at[1] + 4096)
        masks_f, _ = sb("masks_f", [P, NLEVEL, P], F32, scan_at[0])
        head_t, _ = sb("head_t", [P, 2, ALL])
        r_cols, _ = sb("r_cols", [P, 2, ALL // P])
        c_cols, _ = sb("c_cols", [P, ND, 2])
        cols, _ = sb("cols", [P, N_COLS])
        mod, _ = sb("mod", [P, 2, NLAYER * NMOD * ND])
        scale_c, _ = sb("scale_c", [P, 2, ND])
        shift_c, _ = sb("shift_c", [P, 2, ND])
        gate_c, _ = sb("gate_c", [P, 2, ND])
        lb_e, _ = sb("lb_e", [P, 4, NLAYER * 2 * NH])
        lb, _ = sb("lb", [P, 2, NLAYER, NH])
        one_lb, _ = sb("one_lb", [P, 2, NLAYER, NH])
        masks, _ = sb("masks", [P, NLEVEL, P], U8)
        ident, _ = sb("ident", [P, P])
        ones, _ = sb("ones", [P, P])
        eps_c, _ = sb("eps_c", [P, 1])
        poolw, _ = sb("poolw", [P, NG, P])
        assert at[0] <= 229344, at[0]

        bank = [stack.enter_context(nc.psum_tensor(f"bank{i}", [P, 512], F32)) for i in range(8)]

        s_raw = [sem(f"raw_landed{i}") for i in range(RING)]
        s_hi = sem("hi_ready")
        s_lo = sem("lo_ready")
        s_used = sem("units_multiplied")
        s_aland = [sem(f"ada_landed{i}") for i in range(2)]
        s_ada = sem("ada_done")
        s_load = sem("start_landed")
        s_cland = sem("c_landed")
        s_ccland = sem("c_columns_landed")
        s_const = sem("ones_written")
        s_silu_c = sem("silu_c_ready")
        s_up_free = sem("up_banks_free")
        s_silu = sem("silu_ready")
        s_hid_hi = sem("hid_hi_ready")
        s_hid_lo = sem("hid_lo_ready")
        s_res = sem("residual_added")
        s_sq = sem("squared")
        s_sqs = sem("squares_summed")
        s_ssq = sem("norm_total")
        s_std = sem("std_ready")
        s_diag = sem("diag_ready")
        s_bc = sem("rstd_spread")
        s_nt = sem("normed")
        s_uhi = sem("u_hi_ready")
        s_ulo = sem("u_lo_ready")
        s_chain = sem("vector_chain")
        s_proj = sem("projection_out")
        s_vout = sem("v_out")
        s_sga = sem("sig_a_out")
        s_prep = sem("operands_ready")
        s_score = sem("scored")
        s_merge = sem("merged")
        s_cross = sem("cross_copied")
        s_av = sem("head_out")
        s_hsq = sem("head_squared")
        s_x1 = sem("head_weighted")
        s_hss = sem("head_total")
        s_hstd = sem("head_std")
        s_hdg = sem("head_diag")
        s_hbc = sem("head_rstd")
        s_at = sem("head_gated")
        s_ahi = sem("a_hi_ready")
        s_head = sem("head_done")
        s_pvo = sem("pv_out")
        s_box = sem("box_landed")
        s_dmm = sem("box_means")
        s_dout = sem("box_out")
        s_pmm = sem("pool_products")
        s_phi = sem("p_hi_ready")
        s_plo = sem("p_lo_ready")
        s_sgb = sem("sig_b_out")
        s_mt = sem("merge_a")
        s_mg = sem("branches_merged")
        s_fin = sem("out_rows")
        s_out = sem("out_stored")

        def view(t, offset, *dims):
            whole = t[:]
            return bass.AP(whole.tensor, offset, [[whole.ap[0][0], P]] + [list(x) for x in dims])

        def streams(ntok):
            return range(ntok // TOK)

        def span(s):
            return slice(s * TOK, (s + 1) * TOK)

        block = stack.enter_context(nc.Block())

        @block.sync
        def _(sp):
            sp.dma_start(c_cols[:], c_cols_in).then_inc(s_ccland, 16)
            for u in range(RING):
                sp.dma_start(raw[:, u, :], weights[u]).then_inc(s_raw[u], 16)
            with sp.Fori(1, N_UNITS // RING) as i:
                for j in range(RING):
                    sp.wait_ge(s_used, i * RING + (j - RING + 1))
                    sp.dma_start(raw[:, j, :], weights[bass.ds(i * RING + j, 1)].rearrange("a p n -> (a p) n")
                                 ).then_inc(s_raw[j], 16)
            for d in range(ND):
                sp.wait_ge(s_fin, d + 1)
                sp.dma_start(out[:, d, :], sig_a[:, d, 0:TOK]).then_inc(s_out, 16)
            sp.wait_ge(s_out, 16 * ND)

        @block.gpsimd
        def _(pool):
            pool.memset(ones[:], 1.0).then_inc(s_const, 1)
            pool.memset(eps_c[:], EPS).then_inc(s_const, 1)
            pool.dma_start(silu_c[:], c_in.partition_broadcast(P)).then_inc(s_cland, 16)
            for n in range(2):
                pool.dma_start(ada_raw[:, n, :], adaw[n]).then_inc(s_aland[n], 16)

            def load(first, count):
                with pool.Fori(first // 2, (first + count) // 2) as i:
                    for j in range(2):
                        pool.wait_ge(s_ada, i * 4 + 2 * j)
                        pool.dma_start(ada_raw[:, j, :], adaw[bass.ds(i * 2 + j, 1)].rearrange("a p n -> (a p) n")
                                       ).then_inc(s_aland[j], 16)

            def mixer_tables(layer):
                pool.wait_ge(s_used, mix_base(layer))
                if layer:
                    pool.wait_ge(s_pmm, NG * layer)
                for s in range(2):
                    pool.dma_start(box[s][:], box_in[s]).then_inc(s_box, 16)
                pool.dma_start(poolw[:], poolw_in[layer]).then_inc(s_box, 16)

            load(2, ADA[(0, "mix")][0] - 2)
            mixer_tables(0)
            load(ADA[(0, "mix")][0], ADA[(1, "mix")][0] - ADA[(0, "mix")][0])
            mixer_tables(1)
            load(*ADA[(1, "mix")])

        @block.tensor
        def _(pe):
            def half(ps, slot, k0, k1, hi, lo, unit_wait, chunk_wait=None, done=False, start=None, stop=None):
                if unit_wait is not None:
                    pe.wait_ge(s_lo, unit_wait - START)
                for k in range(k0, k1):
                    if chunk_wait is not None:
                        pe.wait_ge(chunk_wait[0], chunk_wait[1] + k + 1)
                    first = k == k0 if start is None else start and k == k0
                    last = k == k1 - 1 if stop is None else stop and k == k1 - 1
                    pe.matmul(ps, w_hi[:, slot, k, :], hi(k), start=first, stop=False)
                    pe.matmul(ps, w_hi[:, slot, k, :], lo(k), start=False, stop=False)
                    mm = pe.matmul(ps, w_lo[:, slot, k, :], hi(k), start=False, stop=last)
                if done:
                    mm.then_inc(s_used, 1)

            def totals(ps, squares, nt):
                for t in range(nt // P):
                    mm = pe.matmul(ps[:, t:t + 1], squares[:, t * P:(t + 1) * P], ones[:, 0:1],
                                   start=True, stop=True)
                return mm

            def norm_total(n):
                nt = norm_tok(n)
                pe.wait_ge(s_sqs, (ND + 1) * (n + 1))
                totals(bank[4], sq_sum, nt).then_inc(s_ssq, 1)
                pe.wait_ge(s_diag, n + 1)
                pe.matmul(bank[5][:, 0:nt], ones[:], view(diag, 0, [1, nt]), start=True, stop=True).then_inc(s_bc, 1)

            def pair(ps, slots, hi, lo, unit, chunk_wait):
                for g in range(2):
                    pe.wait_ge(s_lo, unit - START + g)
                for k in range(ND):
                    if chunk_wait is not None:
                        pe.wait_ge(chunk_wait[0], chunk_wait[1] + k + 1)
                    for p_, slot in zip(ps, slots):
                        pe.matmul(p_, w_hi[:, slot, k, :], hi(k), start=(k == 0), stop=False)
                        pe.matmul(p_, w_hi[:, slot, k, :], lo(k), start=False, stop=False)
                        mm = pe.matmul(p_, w_lo[:, slot, k, :], hi(k), start=False, stop=(k == ND - 1))
                        if k == ND - 1:
                            mm.then_inc(s_used, 1)

            def ffn(layer, which, n_norm):
                ntok = ffn_tok(layer, which)
                hi, lo = (lambda k: u_hi[:, k, 0:ntok]), (lambda k: u_lo[:, k, 0:ntok])
                hh, hl = (lambda k: hid_hi[:, k, 0:ntok]), (lambda k: hid_lo[:, k, 0:ntok])
                norm_total(n_norm)
                base = ffn_base(layer, which)
                hid, res = hid_count(layer, which), res_count(layer, which)
                for part, n in enumerate(PARTS):
                    with pe.Fori(0, n // 2) as i:
                        for b in range(2):
                            pe.wait_ge(s_up_free, i * 2 + (hid + b + 1))
                            if b == 0:
                                pair((bank[0][:, 0:ntok], bank[1][:, 0:ntok]), (0, 1), hi, lo, i * 4 + (base + 1),
                                     (s_ulo, u_count(n_norm)) if part == 0 else None)
                                continue
                            for j in (2, 3):
                                half(bank[j][:, 0:ntok], j, 0, ND, hi, lo, i * 4 + (base + j + 1), done=True)
                    base += 2 * n
                    with pe.Fori(0, ND // 4) as i:
                        for j in range(4):
                            pe.wait_ge(s_res, i * 4 + (res + j + 1))
                            half(bank[4 + j][:, 0:ntok], j % RING, 0, n, hh, hl, i * 4 + (base + j + 1),
                                 (s_hid_lo, hid) if j == 0 else None, done=True)
                    base += ND
                    hid += n
                    res += ND

            def scan_step(layer, head, step):
                n = layer * NH + head
                Sh = S[head % 2]
                ps = bank[6 if step == STEP_STATE else 4 + step % 2]
                pe.wait_ge(s_prep, NSTEP * n + step + 1)
                tiles = range(2 * (ffn_tok(layer, 1) // TOK))
                if step == STEP_STATE:
                    for a in range(2):
                        k0 = TOK + a * P
                        pe.matmul(ps[:, a * TOK:(a + 1) * TOK], Sh[:, 0, k0:k0 + P], Sh[:, 2, 0:TOK],
                                  start=True, stop=False)
                        mm = pe.matmul(ps[:, a * TOK:(a + 1) * TOK], Sh[:, 3, k0:k0 + P], Sh[:, 1, 0:TOK],
                                       start=False, stop=True)
                elif step == STEP_CROSS:
                    for t in tiles:
                        here, there = t * P, (t ^ 1) * P
                        key, query = (0, 2) if t % 2 == 0 else (3, 1)
                        mm = pe.matmul(ps[:, here:here + P], Sh[:, key, here:here + P],
                                       Sh[:, query, there:there + P], start=True, stop=True)
                else:
                    for t in tiles:
                        if step == 0:
                            mm = pe.matmul(ps[:, t * P:(t + 1) * P], Sh[:, 2, t * P:(t + 1) * P],
                                           Sh[:, 1, t * P:(t + 1) * P], start=True, stop=True)
                            continue
                        hb = 1 << (step - 1)
                        for key, query, side in ((0, 2, hb), (3, 1, 0)):
                            cut = [2 * hb, P // (2 * hb)], [1, hb]
                            mm = pe.matmul(view(ps, t * P + side, *cut), Sh[:, key, t * P:(t + 1) * P],
                                           view(Sh, query * ALL + t * P + side, *cut), start=True, stop=True)
                mm.then_inc(s_score, 1)

            def head_out(layer, head):
                n = layer * NH + head
                par = head % 2
                vh = lambda tile: v[:, tile, head * P:(head + 1) * P]
                pe.wait_ge(s_merge, (NLEVEL + 1) * (n + 1))
                pe.wait_ge(s_cross, 2 * (n + 1))
                pe.wait_ge(s_proj, 6 * (n + 1))
                o = bank[7]
                for a in range(2):
                    pe.matmul(o[:, 0:TOK], vh(a), A[par][:, 0, a * TOK:(a + 1) * TOK], start=(a == 0), stop=False)
                for a in range(2):
                    mm = pe.matmul(o[:, 0:TOK], vh(2 + a), AX[par][:, a, :], start=False, stop=(a == 1))
                if ffn_tok(layer, 1) == ALL:
                    for a in range(2):
                        mm = pe.matmul(o[:, TOK:ALL], vh(2 + a), A[par][:, 1, a * TOK:(a + 1) * TOK],
                                       start=(a == 0), stop=(a == 1))
                mm.then_inc(s_av, 1)

            def head_total(layer, head):
                n = layer * NH + head
                pe.wait_ge(s_hsq, n + 1)
                totals(bank[6], head_t[:, 0, :], ffn_tok(layer, 1)).then_inc(s_hss, 1)

            def head_spread(layer, head):
                n = layer * NH + head
                nt = ffn_tok(layer, 1)
                pe.wait_ge(s_hdg, n + 1)
                pe.matmul(bank[6][:, 0:nt], ones[:], head_t[:, 0, 0:nt], start=True, stop=True).then_inc(s_hbc, 1)

            def natural(ps0, unit, j, ntile, half_of=(0, 2), u_wait=None):
                slot = unit % RING
                if half_of[0] == 0:
                    pe.wait_ge(s_lo, unit + 1 - START)
                for kk in range(*half_of):
                    k = 2 * j + kk
                    if u_wait is not None:
                        pe.wait_ge(s_ulo, u_wait + k + 1)
                    wh = view(w_hi, slot * UNIT + kk * 512, [1, 512])
                    wl = view(w_lo, slot * UNIT + kk * 512, [1, 512])
                    for t in range(ntile):
                        ts = slice(t * P, (t + 1) * P)
                        pe.matmul(bank[ps0 + t][:], u_hi[:, k, ts], wh, start=(k == 0), stop=False)
                        pe.matmul(bank[ps0 + t][:], u_hi[:, k, ts], wl, start=False, stop=False)
                        mm = pe.matmul(bank[ps0 + t][:], u_lo[:, k, ts], wh, start=False, stop=(k == ND - 1))
                if half_of[1] == 2:
                    mm.then_inc(s_used, 1)

            def mixer(layer, n_norm):
                nt = ffn_tok(layer, 1)
                ntile = nt // P
                hi = lambda m: (lambda k: u_hi[:, k, 0:m])
                lo = lambda m: (lambda k: u_lo[:, k, 0:m])
                unit = mix_base(layer)
                n0 = layer * NH
                norm_total(n_norm)
                pe.wait_ge(s_res, res_count(layer, 0) + 4 + 3 * ND)
                for j in range(4):
                    natural(0, unit + j, j, 4, u_wait=u_count(n_norm))
                unit += 4
                for j in range(4):
                    m = nt if j in (0, 3) else ALL
                    half(bank[4 + j][:, 0:m], j % RING, 0, ND, hi(m), lo(m), unit + j + 1, done=True)
                unit += 4
                for head in range(NH):
                    n = n0 + head
                    for piece in range(12):
                        j, second = piece // 2, piece % 2
                        k0 = 4 * second
                        if head < NH - 1 or j < 2:
                            if head < NH - 1:
                                m = nt if j in (0, 3, 4, 5) else ALL
                                b = j % 4
                            else:
                                m, b = nt, j
                            if not second:
                                if head == 0 and j == 0:
                                    pe.wait_ge(s_vout, layer + 1)
                                elif head < NH - 1 and j in (0, 1):
                                    pe.wait_ge(s_sga, layer * ND + 2 * head - 1 + j)
                                elif head < NH - 1 and j in (2, 3):
                                    pe.wait_ge(s_proj, 6 * (n + 1))
                                elif head < NH - 1 and j == 4:
                                    pe.wait_ge(s_proj, 6 * (n + 1) + 1)
                                elif head < NH - 1 and j == 5:
                                    pe.wait_ge(s_proj, 6 * (n + 1) + 3)
                                else:
                                    pe.wait_ge(s_proj, 6 * (n + 1))
                                    pe.wait_ge(s_sga, layer * ND + 2 * head - 1 + j)
                            half(bank[b][:, 0:m], (unit + j) % RING, k0, k0 + 4, hi(m), lo(m),
                                 unit + j + 1 if not second else None, done=bool(second),
                                 start=not second, stop=bool(second))
                        else:
                            if j == 2 and not second:
                                pe.wait_ge(s_sga, layer * ND + ND)
                            natural(0, unit + j, j - 2, ntile, (second, second + 1))
                        if piece < NSTEP:
                            scan_step(layer, head, piece)
                            if piece == 1 and head:
                                head_spread(layer, head - 1)
                        elif piece == NSTEP:
                            head_out(layer, head)
                        else:
                            head_total(layer, head)
                    unit += 6
                head_spread(layer, NH - 1)
                pe.wait_ge(s_box, 48 * (layer + 1))
                pe.wait_ge(s_pvo, layer + 1)
                for g in range(NG):
                    for s in streams(nt):
                        for a in range(2):
                            mm = pe.matmul(bank[g][:, span(s)], pv[:, 2 * s + a, g * P:(g + 1) * P],
                                           box[s][:, a, g, :], start=(a == 0), stop=(a == 1))
                    mm.then_inc(s_dmm, 1)
                pe.wait_ge(s_head, n0 + NH)
                for g in range(NG):
                    pe.wait_ge(s_dout, layer * NG + g + 1)
                    pe.matmul(bank[4 + g][:, 0:nt], poolw[:, g, :], dpool[:, g, 0:nt],
                              start=True, stop=True).then_inc(s_pmm, 1)
                pe.wait_ge(s_plo, (layer + 1) * NG)
                with pe.Fori(0, ND // 2) as i:
                    for b in range(2):
                        pe.wait_ge(s_mg, i * 2 + (layer * ND + b + 1))
                        half(bank[4 * b][:, 0:nt], 2 * b, 0, ND, hi(nt), lo(nt), i * 4 + (unit + 2 * b + 1), done=True)
                        half(bank[4 * b + 1][:, 0:nt], 2 * b + 1, 0, 4, lambda k: a_hi[:, k, 0:nt],
                             lambda k: a_lo[:, k, 0:nt], i * 4 + (unit + 2 * b + 2))
                        half(bank[4 * b + 2][:, 0:nt], 2 * b + 1, 4, 8, lambda k: p_hi[:, k - 4, 0:nt],
                             lambda k: p_lo[:, k - 4, 0:nt], None, done=True)
                unit += 2 * ND
                res = res_count(layer, 0) + 3 * ND
                with pe.Fori(0, ND // 4) as i:
                    for j in range(4):
                        if j == 0:
                            pe.wait_ge(s_mg, layer * ND + ND + 2)
                        pe.wait_ge(s_res, i * 4 + (res + j + 1))
                        half(bank[4 + j][:, 0:nt], j % RING, 0, ND, hi(nt), lo(nt), i * 4 + (unit + j + 1),
                             (s_ulo, u_count(n_norm) + ND) if j == 0 else None, done=True)

            pe.wait_ge(s_silu_c, 1)
            with pe.Fori(0, START // RING) as i:
                for j in range(RING):
                    pe.wait_ge(s_raw[j], i * 16 + 16)
                    for k in range(ND):
                        mm = pe.matmul(bank[6][:, bass.ds(i * 8 + 2 * j, 2)],
                                       raw[:, j, k * P:(k + 1) * P], c_cols[:, k, :], start=(k == 0), stop=(k == ND - 1))
                    mm.then_inc(s_used, 1)
            pe.wait_ge(s_const, 2)
            n_norm = 0
            for layer in range(NLAYER):
                ffn(layer, 0, n_norm)
                mixer(layer, n_norm + 1)
                ffn(layer, 1, n_norm + 2)
                n_norm += 3
            norm_total(n_norm)

        @block.scalar
        def _(act):
            def split_next(base, i, j):
                act.wait_ge(s_used, i * 4 + (base + j - RING + 1) if i is not None else base + j - RING + 1)
                act.wait_ge(s_raw[j % RING], (i + (base + j) // 4 + 1) * 16 if i is not None
                            else ((base + j) // 4 + 1) * 16)
                act.activation(view(w_hi, (j % RING) * UNIT, [1, UNIT]), raw[:, j % RING, :], ACT.Copy
                               ).then_inc(s_hi, 1)

            def square(n, i, d, res):
                nt = norm_tok(n)
                at4 = (lambda x: i * 4 + x) if i is not None else (lambda x: x)
                act.wait_ge(s_res, at4(4 + res + d + 1))
                if n or d:
                    act.wait_ge(s_sqs, at4((ND + 1) * n + d))
                src = h[:, bass.ds(at4(d), 1), 0:nt].rearrange("p a n -> p (a n)")
                act.activation(sq[:, d % 2, 0:nt], src, ACT.Square).then_inc(s_sq, 1)

            def norm(n, to_u=True):
                nt = norm_tok(n)
                act.wait_ge(s_ssq, n + 1)
                act.activation(r_cols[:, 0, 0:nt // P], bank[4][:, 0:nt // P], ACT.Sqrt, bias=eps_c[:], scale=1.0 / D
                               ).then_inc(s_std, 1)
                if not to_u:
                    return
                for d in range(ND):
                    act.wait_ge(s_nt, 8 * n + d + 1)
                    for s in streams(nt):
                        ins = act.activation(u_hi[:, d, span(s)], norm_t[:, d % 4, span(s)], ACT.Identity,
                                             bias=shift_c[:, s, d:d + 1])
                    ins.then_inc(s_uhi, 1)

            def ffn(layer, which, n_norm):
                nt = ffn_tok(layer, which)
                norm(n_norm)
                base = ffn_base(layer, which)
                hid = hid_count(layer, which)
                last_ffn = layer == NLAYER - 1 and which == 1
                for part, n in enumerate(PARTS):
                    with act.Fori(0, n // 2) as i:
                        for b in range(2):
                            split_next(base, i, 2 * b + AHEAD)
                            split_next(base, i, 2 * b + AHEAD + 1)
                            act.wait_ge(s_used, i * 4 + (base + 2 * b + 2))
                            act.activation(silu_t[:, b, 0:nt], bank[2 * b][:, 0:nt], ACT.Silu).then_inc(s_silu, 1)
                            act.wait_ge(s_up_free, i * 2 + (hid + b + 3))
                            act.activation(hid_hi[:, bass.ds(i * 2 + b, 1), 0:nt].rearrange("p a n -> p (a n)"),
                                           hid_t[:, b, 0:nt], ACT.Copy).then_inc(s_hid_hi, 1)
                    base += 2 * n
                    hid += n
                    rounds = ND // 4
                    if last_ffn and part == len(PARTS) - 1:
                        rounds -= 1
                    to_norm = part == len(PARTS) - 1
                    res = res_count(layer, which) + part * ND
                    with act.Fori(0, rounds) as i:
                        for j in range(4):
                            split_next(base, i, j + AHEAD)
                            if to_norm:
                                square(n_norm + 1, i, j, res)
                    if rounds < ND // 4:
                        split_next(base + 4 * rounds, None, AHEAD)
                        for j in range(4):
                            square(n_norm + 1, None, 4 * rounds + j, res)
                    base += ND

            def proj(layer, head, which, ps, nt):
                par = head % 2
                if which == 0:
                    if layer * NH + head >= 2:
                        act.wait_ge(s_x1, layer * NH + head - 1)
                    act.activation(S[par][:, 1, 0:nt], ps[:, 0:nt], ACT.Silu).then_inc(s_proj, 1)
                elif which == 3:
                    act.activation(gs[:, par, 0:nt], ps[:, 0:nt], ACT.Silu).then_inc(s_proj, 1)
                else:
                    act.activation(T[par][:, which - 1, :], ps[:], ACT.Sigmoid).then_inc(s_proj, 1)
                    act.activation(S[par][:, 0 if which == 1 else 3, :], ps[:], ACT.Sigmoid, scale=-1.0
                                   ).then_inc(s_proj, 1)

            def head_std(n, nt):
                act.wait_ge(s_hss, n + 1)
                act.activation(r_cols[:, 1, 0:nt // P], bank[6][:, 0:nt // P], ACT.Sqrt, bias=eps_c[:],
                               scale=1.0 / P).then_inc(s_hstd, 1)

            def head_hi(layer, head, nt):
                act.wait_ge(s_at, layer * NH + head + 1)
                act.activation(a_hi[:, head, 0:nt], head_t[:, 1, 0:nt], ACT.Copy).then_inc(s_ahi, 1)

            def mixer(layer, n_norm):
                nt = ffn_tok(layer, 1)
                base = mix_base(layer)
                norm(n_norm)
                for j in range(4):
                    if j == 3:
                        split_next(base, None, j + AHEAD)
                        act.wait_ge(s_used, base + 4)
                        for t in range(4):
                            ins = act.activation(v[:, t, :], bank[t][:], ACT.Copy)
                        ins.then_inc(s_vout, 1)
                    else:
                        split_next(base, None, j + AHEAD)
                base += 4
                for j in range(4):
                    split_next(base, None, j + AHEAD)
                    act.wait_ge(s_used, base + j + 1)
                    proj(layer, 0, j, bank[4 + j], nt if j in (0, 3) else ALL)
                base += 4
                for head in range(NH):
                    n = layer * NH + head
                    par = head % 2
                    for piece in range(12):
                        j = piece // 2
                        if piece % 2:
                            split_next(base + j - (base + j) % 4, None, (base + j) % 4 + AHEAD)
                            act.wait_ge(s_used, base + j + 1)
                            if head < NH - 1:
                                if j < 4:
                                    proj(layer, head + 1, j, bank[j], nt if j in (0, 3) else ALL)
                                else:
                                    act.activation(sig_a[:, 2 * head + j - 4, 0:nt], bank[j - 4][:, 0:nt],
                                                   ACT.Sigmoid).then_inc(s_sga, 1)
                            elif j < 2:
                                act.activation(sig_a[:, 2 * head + j, 0:nt], bank[j][:, 0:nt], ACT.Sigmoid
                                               ).then_inc(s_sga, 1)
                        if piece == 2 and head:
                            head_hi(layer, head - 1, nt)
                        if piece == STEP_CROSS:
                            act.wait_ge(s_score, NSTEP * n + STEP_CROSS + 1)
                            for s in streams(nt):
                                ins = act.activation(A[par][:, s, P:3 * P], bank[4][:, span(s)], ACT.Copy)
                            ins.then_inc(s_cross, 1)
                        elif piece == STEP_STATE:
                            act.wait_ge(s_score, NSTEP * n + STEP_STATE + 1)
                            act.activation(AX[par][:], bank[6][:].rearrange("p (a t) -> p a t", a=2), ACT.Copy
                                           ).then_inc(s_cross, 1)
                        elif piece == NSTEP:
                            act.wait_ge(s_av, n + 1)
                            if n:
                                act.wait_ge(s_head, n)
                            act.activation(head_t[:, 0, 0:nt], bank[7][:, 0:nt], ACT.Square).then_inc(s_hsq, 1)
                        elif piece == NSTEP + 1:
                            head_std(n, nt)
                    base += 6
                for t in range(nt // P):
                    ins = act.activation(pv[:, t, :], bank[t][:], ACT.Copy)
                ins.then_inc(s_pvo, 1)
                head_hi(layer, NH - 1, nt)
                for g in range(NG):
                    act.wait_ge(s_dmm, layer * NG + g + 1)
                    act.activation(dpool[:, g, 0:nt], bank[g][:, 0:nt], ACT.Copy).then_inc(s_dout, 1)
                psc = lambda g: cols[:, C_PSC + layer * NG + g:C_PSC + layer * NG + g + 1]
                for g in range(NG):
                    act.wait_ge(s_pmm, layer * NG + g + 1)
                    act.activation(p_hi[:, g, 0:nt], bank[4 + g][:, 0:nt], ACT.Copy, scale=psc(g)).then_inc(s_phi, 1)
                with act.Fori(0, ND // 2) as i:
                    for b in range(2):
                        split_next(base, i, 2 * b + AHEAD)
                        act.wait_ge(s_used, i * 4 + (base + 2 * b + 1))
                        act.wait_ge(s_mg, i * 2 + (layer * ND + b + 1))
                        act.activation(sig_b[:, b, 0:nt], bank[4 * b][:, 0:nt], ACT.Sigmoid).then_inc(s_sgb, 1)
                        split_next(base, i, 2 * b + AHEAD + 1)
                base += 2 * ND
                act.wait_ge(s_used, base)
                for d in range(ND):
                    act.wait_ge(s_mg, layer * ND + d + 3)
                    act.activation(u_hi[:, d, 0:nt], sig_a[:, d, 0:nt], ACT.Copy).then_inc(s_uhi, 1)
                with act.Fori(0, ND // 4) as i:
                    for j in range(4):
                        split_next(base, i, j + AHEAD)
                        square(n_norm + 1, i, j, res_count(layer, 0) + len(PARTS) * ND)

            act.dma_start(cols[:], cols_in).then_inc(s_load, 16)
            act.dma_start(h[:], resid_in).then_inc(s_load, 16)
            act.dma_start(ident[:], ident_in).then_inc(s_load, 16)
            act.dma_start(masks_f[:], masks_in).then_inc(s_load, 16)
            act.wait_ge(s_ccland, 16)
            act.activation(c_cols[:], c_cols[:], ACT.Silu).then_inc(s_silu_c, 1)
            act.wait_ge(s_cland, 16)
            act.activation(silu_c[:], silu_c[:], ACT.Silu).then_inc(s_silu_c, 1)
            act.wait_ge(s_load, 64)
            act.wait_ge(s_chain, 2 + NLAYER)
            act.activation(lb_e[:, 1, :], lb_e[:, 0, :], ACT.Exp).then_inc(s_silu_c, 1)
            for d in range(ND):
                square(0, None, d, -d - 1)
            act.wait_ge(s_const, 2)
            for j in range(AHEAD):
                split_next(START, None, j)
            n_norm = 0
            for layer in range(NLAYER):
                ffn(layer, 0, n_norm)
                mixer(layer, n_norm + 1)
                ffn(layer, 1, n_norm + 2)
                n_norm += 3
            norm(n_norm, to_u=False)

        @block.vector
        def _(dve):
            chain = [0]

            def link(ins):
                chain[0] += 1
                ins.then_inc(s_chain, 1)
                dve.wait_ge(s_chain, chain[0])

            def split_lo(base, i, j):
                dve.wait_ge(s_hi, i * 4 + (base + j + 1 - START) if i is not None else base + j + 1 - START)
                dve.tensor_tensor(view(w_lo, (j % RING) * UNIT, [1, UNIT]), raw[:, j % RING, :],
                                  view(w_hi, (j % RING) * UNIT, [1, UNIT]).bitcast(F32), ALU.subtract
                                  ).then_inc(s_lo, 1)

            def ada_pair(pair, first):
                for j in range(2):
                    dve.wait_ge(s_aland[j], (pair + first // 2 + 1) * 16)
                    for s in range(2):
                        dve.wait_ge(s_ada, pair * 4 + (2 * (first + j) + s + 1))
                        dve.scalar_tensor_tensor(
                            out=junk[:, s, :], in0=ada_raw[:, j, :], scalar=1.0, in1=silu_c[:, s, :],
                            op0=ALU.mult, op1=ALU.mult,
                            accum_out=mod[:, s, bass.ds(pair * 2 + (START + first + j), 1)]).then_inc(s_ada, 1)

            def column(t, k, layer):
                return view(cols, C_ADAB + (layer * NMOD + k) * ND, [0, 2], [1, ND])

            def mod_of(layer, k):
                at0 = (layer * NMOD + k) * ND
                return mod[:, :, at0:at0 + ND]

            def norm_columns(layer, k0, norm_i):
                if layer or k0:
                    dve.wait_ge(s_ada, 2 + 2 * ((layer * NMOD + k0 + 2) * ND - START))
                link(dve.tensor_tensor(scale_c[:], mod_of(layer, k0 + 1), column(cols, k0 + 1, layer), ALU.add))
                link(dve.scalar_tensor_tensor(out=scale_c[:], in0=scale_c[:], scalar=1.0,
                                              in1=view(cols, C_NORM + (layer * 3 + norm_i) * ND, [0, 2], [1, ND]),
                                              op0=ALU.add, op1=ALU.mult))
                link(dve.tensor_tensor(shift_c[:], mod_of(layer, k0), column(cols, k0, layer), ALU.add))

            def gate_columns(layer, k, factor):
                dve.wait_ge(s_ada, 2 + 2 * ((layer * NMOD + k + 1) * ND - START))
                link(dve.tensor_tensor(gate_c[:], mod_of(layer, k), column(cols, k, layer), ALU.add))
                link(dve.tensor_scalar(gate_c[:], gate_c[:], factor, None, ALU.mult))

            def spread(std, into, offset, nt):
                link(dve.reciprocal(std, std))
                tiles = nt // P
                cell_at = bass.AP(std.tensor, std.offset, [list(std.ap[0]), [1, tiles], [0, P]])
                return dve.tensor_tensor(view(into, offset, [P, tiles], [1, P]),
                                         view(ident, 0, [0, tiles], [1, P]), cell_at, ALU.mult)

            def clear_sum(n):
                dve.memset(sq_sum[:, 0:norm_tok(n)], 0.0).then_inc(s_sqs, 1)

            def add_squares(n, i, d):
                nt = norm_tok(n)
                at4 = (lambda x: i * 4 + x) if i is not None else (lambda x: x)
                dve.wait_ge(s_sq, at4(ND * n + d + 1))
                dve.wait_ge(s_sqs, at4((ND + 1) * n + d + 1))
                dve.tensor_tensor(sq_sum[:, 0:nt], sq_sum[:, 0:nt], sq[:, d % 2, 0:nt], ALU.add).then_inc(s_sqs, 1)

            def norm(n, to_u=True):
                nt = norm_tok(n)
                dve.wait_ge(s_std, n + 1)
                spread(r_cols[:, 0, 0:nt // P], diag, 0, nt).then_inc(s_diag, 1)
                dve.wait_ge(s_bc, n + 1)
                if not to_u:
                    for d in range(ND):
                        dve.scalar_tensor_tensor(out=sig_a[:, d, 0:nt], in0=h[:, d, 0:nt],
                                                 scalar=cols[:, C_FIN + d:C_FIN + d + 1], in1=bank[5][:, 0:nt],
                                                 op0=ALU.mult, op1=ALU.mult).then_inc(s_fin, 1)
                    return

                def scaled(d):
                    for s in streams(nt):
                        ins = dve.scalar_tensor_tensor(out=norm_t[:, d % 4, span(s)], in0=h[:, d, span(s)],
                                                       scalar=scale_c[:, s, d:d + 1], in1=bank[5][:, span(s)],
                                                       op0=ALU.mult, op1=ALU.mult)
                    ins.then_inc(s_nt, 1)

                def low(d):
                    dve.wait_ge(s_uhi, u_count(n) + d + 1)
                    for s in streams(nt):
                        ins = dve.scalar_tensor_tensor(out=u_lo[:, d, span(s)], in0=norm_t[:, d % 4, span(s)],
                                                       scalar=shift_c[:, s, d:d + 1],
                                                       in1=u_hi[:, d, span(s)].bitcast(F32),
                                                       op0=ALU.add, op1=ALU.subtract)
                    ins.then_inc(s_ulo, 1)

                for d in range(ND):
                    scaled(d)
                    if d:
                        low(d - 1)
                low(ND - 1)

            def residual(d, ps, nt):
                for s in streams(nt):
                    hd = h[:, bass.ds(d, 1), span(s)].rearrange("p a n -> p (a n)")
                    ins = dve.scalar_tensor_tensor(
                        out=hd, in0=ps[:, span(s)],
                        scalar=gate_c[:, s, bass.ds(d, 1)], in1=hd, op0=ALU.mult, op1=ALU.add)
                ins.then_inc(s_res, 1)

            def ffn(layer, which, n_norm):
                nt = ffn_tok(layer, which)
                k0 = 6 * which
                norm_columns(layer, k0, 2 * which)
                norm(n_norm)
                base = ffn_base(layer, which)
                hid = hid_count(layer, which)
                last_ffn = layer == NLAYER - 1 and which == 1
                ada_at = ADA.get((layer, f"ffn{which}"), (None, 0))[0]
                for part, n in enumerate(PARTS):
                    with dve.Fori(0, n // 2) as i:
                        for b in range(2):
                            split_lo(base, i, 2 * b + AHEAD)
                            split_lo(base, i, 2 * b + AHEAD + 1)
                            dve.wait_ge(s_silu, i * 2 + (hid + b + 1))
                            dve.tensor_tensor(hid_t[:, b, 0:nt], silu_t[:, b, 0:nt], bank[2 * b + 1][:, 0:nt],
                                              ALU.mult).then_inc(s_up_free, 1)
                            dve.wait_ge(s_hid_hi, i * 2 + (hid + b + 1))
                            f = i * 2 + b
                            dve.tensor_tensor(
                                hid_lo[:, bass.ds(f, 1), 0:nt].rearrange("p a n -> p (a n)"), hid_t[:, b, 0:nt],
                                hid_hi[:, bass.ds(f, 1), 0:nt].rearrange("p a n -> p (a n)").bitcast(F32),
                                ALU.subtract).then_inc(s_hid_lo, 1)
                        if ada_at is not None:
                            ada_pair(i, ada_at)
                    base += 2 * n
                    hid += n
                    if ada_at is not None:
                        ada_at += n
                    if part == 0:
                        gate_columns(layer, k0 + 2, 0.5)
                    rounds = ND // 4
                    final = last_ffn and part == len(PARTS) - 1
                    if final:
                        rounds -= 1
                    to_norm = part == len(PARTS) - 1
                    if to_norm:
                        clear_sum(n_norm + 1)
                    with dve.Fori(0, rounds) as i:
                        for j in range(4):
                            dve.wait_ge(s_used, i * 4 + (base + j + 1))
                            residual(i * 4 + j, bank[4 + j], nt)
                            split_lo(base, i, j + AHEAD)
                            if to_norm:
                                add_squares(n_norm + 1, i, j)
                        if ada_at is not None:
                            ada_pair(i, ada_at)
                    if final:
                        for j in range(4):
                            dve.wait_ge(s_used, base + 4 * rounds + j + 1)
                            residual(4 * rounds + j, bank[4 + j], nt)
                            if j == 0:
                                split_lo(base + 4 * rounds, None, AHEAD)
                            add_squares(n_norm + 1, None, 4 * rounds + j)
                    base += ND
                    if ada_at is not None:
                        ada_at += ND // 2

            def prepare_head(layer, head):
                par = head % 2
                n = layer * NH + head
                lb_of = lambda d: lb[:, d, layer, head:head + 1]
                one_of = lambda d: one_lb[:, d, layer, head:head + 1]
                dve.wait_ge(s_proj, 6 * n + 5)
                for d in range(2):
                    dve.tensor_scalar(T[par][:, d, :], T[par][:, d, :], one_of(d), lb_of(d), ALU.mult, ALU.add)
                    key = S[par][:, 3 * d, :]
                    ins = dve.tensor_scalar(key, key, one_of(d), None, ALU.mult)
                link(ins)
                nt = ffn_tok(layer, 1)
                dve.tensor_tensor(S[par][:, 2, 0:nt], S[par][:, 0, 0:nt], S[par][:, 3, 0:nt], ALU.add
                                  ).then_inc(s_prep, 1)

            def prepare_step(n, step):
                Sh, Th = S[n % 2], T[n % 2]
                nt = ffn_tok(n // NH, 1)
                if step == 1:
                    link(dve.tensor_tensor(Sh[:, 2, 0:nt], Sh[:, 1, 0:nt], Th[:, 0, 0:nt], ALU.mult))
                    dve.tensor_tensor(Sh[:, 1, 0:nt], Sh[:, 1, 0:nt], Th[:, 1, 0:nt], ALU.mult).then_inc(s_prep, 1)
                    return
                hb = 1 << (step - 2)
                nb = ALL // (2 * hb)

                def carry(array, arrays, side, tokens, d):
                    at0 = array * ALL + side * hb
                    cut = [ALL, arrays], [2 * hb, tokens // (2 * hb)]
                    t = view(Sh, at0, *cut, [1, hb])
                    return dve.tensor_tensor(t, t, view(Th, d * ALL + (1 - side) * hb, *cut, [0, hb]), ALU.mult)

                if nt == ALL:
                    carry(0, 2, 0, ALL, 0)
                else:
                    carry(0, 1, 0, ALL, 0)
                    carry(1, 1, 0, nt, 1)
                if nt == ALL:
                    ins = carry(2, 2, 1, ALL, 0)
                else:
                    carry(2, 1, 1, nt, 0)
                    ins = carry(3, 1, 1, ALL, 1)
                ins.then_inc(s_prep, 1)

            def double_totals(n, step):
                hb = 1 << (step - 2)
                dve.wait_ge(s_prep, NSTEP * n + step + 1)
                both = lambda side: view(T[n % 2], side * hb, [ALL, 2], [2 * hb, ALL // (2 * hb)])
                link(dve.tensor_tensor(both(0), both(0), both(1), ALU.mult))

            def head_diag(n, nt):
                dve.wait_ge(s_hstd, n + 1)
                spread(r_cols[:, 1, 0:nt // P], head_t, 0, nt).then_inc(s_hdg, 1)

            def head_gate(n, nt):
                dve.wait_ge(s_hbc, n + 1)
                dve.tensor_tensor(head_t[:, 1, 0:nt], head_t[:, 1, 0:nt], bank[6][:, 0:nt], ALU.mult
                                  ).then_inc(s_at, 1)

            def head_lo(layer, head, nt):
                dve.wait_ge(s_ahi, layer * NH + head + 1)
                dve.tensor_tensor(a_lo[:, head, 0:nt], head_t[:, 1, 0:nt], a_hi[:, head, 0:nt].bitcast(F32),
                                  ALU.subtract).then_inc(s_head, 1)

            def merge(layer, head, step):
                par = head % 2
                ns = ffn_tok(layer, 1) // TOK
                dst = view(A[par], 0, [2 * TOK, ns], [TOK + P, 2], [1, P])
                src = view(bank[4 + step % 2], 0, [2 * P, ns], [P, 2], [1, P])
                if step == 0:
                    dve.tensor_tensor(dst, src, view(ident, 0, [0, ns], [0, 2], [1, P]), ALU.mult).then_inc(s_merge, 1)
                else:
                    dve.copy_predicated(dst, view(masks, (step - 1) * P, [0, ns], [0, 2], [1, P]), src
                                        ).then_inc(s_merge, 1)

            def mixer(layer, n_norm):
                nt = ffn_tok(layer, 1)
                base = mix_base(layer)
                n0 = layer * NH
                norm_columns(layer, 3, 1)
                norm(n_norm)
                gate_columns(layer, 5, 1.0)
                for j in range(8):
                    split_lo(base, None, j + AHEAD)
                    if layer and j == 0:
                        ada_pair(0, ADA[(1, "mix")][0])
                base += 8
                prepare_head(layer, 0)
                for head in range(NH):
                    n = n0 + head
                    par = head % 2
                    for piece in range(12):
                        if piece % 2:
                            j = piece // 2
                            split_lo(base + j - (base + j) % 4, None, (base + j) % 4 + AHEAD)
                        if piece < NSTEP:
                            dve.wait_ge(s_score, NSTEP * n + piece + 1)
                            if piece < NSTEP - 1:
                                dve.wait_ge(s_prep, NSTEP * n + piece + 1)
                                if 1 <= piece <= NLEVEL + 1:
                                    dve.wait_ge(s_merge, (NLEVEL + 1) * n + piece)
                                prepare_step(n, piece + 1)
                            if piece <= NLEVEL:
                                merge(layer, head, piece)
                            if 1 <= piece <= NLEVEL:
                                double_totals(n, piece + 1)
                            if head and piece == 0:
                                head_diag(n - 1, nt)
                            if head and piece == 2:
                                head_gate(n - 1, nt)
                            if head and piece == 3:
                                head_lo(layer, head - 1, nt)
                        elif piece == NSTEP:
                            if head < NH - 1:
                                prepare_head(layer, head + 1)
                        else:
                            dve.wait_ge(s_av, n + 1)
                            dve.wait_ge(s_proj, 6 * (n + 1))
                            dve.wait_ge(s_hsq, n + 1)
                            hgw = cols[:, C_HGW + layer * NH + head:C_HGW + layer * NH + head + 1]
                            dve.scalar_tensor_tensor(out=head_t[:, 1, 0:nt], in0=bank[7][:, 0:nt], scalar=hgw,
                                                     in1=gs[:, par, 0:nt], op0=ALU.mult, op1=ALU.mult
                                                     ).then_inc(s_x1, 1)
                    base += 6
                head_diag(n0 + NH - 1, nt)
                head_gate(n0 + NH - 1, nt)
                head_lo(layer, NH - 1, nt)
                psc = lambda g: cols[:, C_PSC + layer * NG + g:C_PSC + layer * NG + g + 1]
                for g in range(NG):
                    dve.wait_ge(s_phi, layer * NG + g + 1)
                    dve.scalar_tensor_tensor(out=p_lo[:, g, 0:nt], in0=bank[4 + g][:, 0:nt], scalar=psc(g),
                                             in1=p_hi[:, g, 0:nt].bitcast(F32), op0=ALU.mult, op1=ALU.subtract
                                             ).then_inc(s_plo, 1)
                ada_at = ADA[(layer, "mix")][0] + 2 * layer
                with dve.Fori(0, ND // 2) as i:
                    for b in range(2):
                        split_lo(base, i, 2 * b + AHEAD)
                        split_lo(base, i, 2 * b + AHEAD + 1)
                        dve.wait_ge(s_used, i * 4 + (base + 2 * b + 2))
                        sa = sig_a[:, bass.ds(i * 2 + b, 1), 0:nt].rearrange("p a n -> p (a n)")
                        dve.tensor_tensor(mix_t[:, b, 0, 0:nt], sa, bank[4 * b + 1][:, 0:nt], ALU.mult)
                        dve.wait_ge(s_sgb, i * 2 + (layer * ND + b + 1))
                        dve.tensor_tensor(mix_t[:, b, 1, 0:nt], sig_b[:, b, 0:nt], bank[4 * b + 2][:, 0:nt],
                                          ALU.mult).then_inc(s_mt, 1)
                        dve.wait_ge(s_mt, i * 2 + (layer * ND + b + 1))
                        dve.tensor_tensor(sa, mix_t[:, b, 0, 0:nt], mix_t[:, b, 1, 0:nt], ALU.add).then_inc(s_mg, 1)
                    ada_pair(i, ada_at)
                ada_at += ND
                base += 2 * ND
                for d in range(ND):
                    dve.wait_ge(s_uhi, u_count(n_norm) + ND + d + 1)
                    dve.tensor_tensor(u_lo[:, d, 0:nt], sig_a[:, d, 0:nt], u_hi[:, d, 0:nt].bitcast(F32),
                                      ALU.subtract).then_inc(s_ulo, 1)
                clear_sum(n_norm + 1)
                with dve.Fori(0, ND // 4) as i:
                    for j in range(4):
                        dve.wait_ge(s_used, i * 4 + (base + j + 1))
                        residual(i * 4 + j, bank[4 + j], nt)
                        split_lo(base, i, j + AHEAD)
                        add_squares(n_norm + 1, i, j)
                    if layer == 0:
                        ada_pair(i * 2, ada_at)
                        ada_pair(i * 2 + 1, ada_at)

            dve.memset(scale_c[:], 0.0).then_inc(s_up_free, 2)
            dve.memset(shift_c[:], 0.0).then_inc(s_res, 4)
            dve.memset(gate_c[:], 0.0).then_inc(s_mg, 2)
            dve.memset(lb[:], 0.0).then_inc(s_ada, 2)
            dve.wait_ge(s_load, 64)
            link(dve.tensor_copy(masks[:], masks_f[:]))
            dve.wait_ge(s_load, 64)
            low = lambda l: view(cols, C_LB + l * NH, [NLAYER * NH, 2], [1, NH])
            cell = lambda t, l: view(lb_e, t * NLAYER * 2 * NH + l * NH, [NLAYER * NH, 2], [1, NH])
            one = lambda t: view(lb_e, t * NLAYER * 2 * NH, [NH, 2], [1, NH])
            link(dve.tensor_tensor(one(2), low(0), low(1), ALU.max))
            for l in range(NLAYER):
                link(dve.tensor_tensor(cell(0, l), low(l), one(2), ALU.subtract))
            dve.wait_ge(s_silu_c, 3)
            link(dve.tensor_tensor(one(3), cell(1, 0), cell(1, 1), ALU.add))
            link(dve.reciprocal(one(3), one(3)))
            for l in range(NLAYER):
                link(dve.tensor_tensor(cell(0, l), cell(1, l), one(3), ALU.mult))
            link(dve.tensor_tensor(lb[:, :, 0, :], cell(0, 0), cell(0, 0), ALU.subtract))
            link(dve.tensor_tensor(lb[:, :, 1, :], cell(0, 0), cell(0, 1), ALU.add))
            link(dve.tensor_tensor(lb[:, :, 1, :], lb[:, :, 1, :], cell(0, 0), ALU.subtract))
            link(dve.tensor_scalar(one_lb[:], lb[:], -1.0, 1.0, ALU.mult, ALU.add))
            clear_sum(0)
            for d in range(ND):
                add_squares(0, None, d)
            for j in range(AHEAD):
                split_lo(START, None, j)
            dve.wait_ge(s_used, START)
            link(dve.tensor_copy(mod[:, :, 0:START], view(bank[6], 0, [1, 2], [2, START])))
            dve.wait_ge(s_silu_c, 2)
            n_norm = 0
            for layer in range(NLAYER):
                ffn(layer, 0, n_norm)
                mixer(layer, n_norm + 1)
                ffn(layer, 1, n_norm + 2)
                n_norm += 3
            norm(n_norm, to_u=False)


def ffn_tok(layer, which):
    return TOK if layer == NLAYER - 1 and which == 1 else ALL


def hid_count(layer, which):
    return (2 * layer + which) * NF


def res_count(layer, which):
    return layer * (2 * len(PARTS) + 1) * ND + which * (len(PARTS) + 1) * ND


def norm_res(n):
    return res_count(n // 3, 0) + (0, len(PARTS) * ND, (len(PARTS) + 1) * ND)[n % 3]


def norm_tok(n):
    return ALL if n < 3 * NLAYER - 1 else TOK


def u_count(n):
    return ND * (n + n // 3 + (n % 3 == 2))


def kernel(x, c, ctx, c_ctx, ada_w, ada_b, norm_w, ffn_wg, ffn_wu, ffn_wd, w_in, lower_bounds,
           hg_norm_w, pool_w, pool_scale, w_branch_a, w_branch_b, w_out, final_norm_w):
    import concourse.bacc as bacc
    from concourse.bass_utils import run_bass_kernel_spmd

    f = lambda a: np.asarray(a)
    x, c, ctx, c_ctx, ada_w, ada_b, norm_w = map(f, (x, c, ctx, c_ctx, ada_w, ada_b, norm_w))
    wg, wu, wd, w_in, lower_bounds = map(f, (ffn_wg, ffn_wu, ffn_wd, w_in, lower_bounds))
    hg_norm_w, pool_w, pool_scale, wa, wb = map(f, (hg_norm_w, pool_w, pool_scale, w_branch_a, w_branch_b))
    w_out, final_norm_w = f(w_out), f(final_norm_w)

    def columns(w):
        return w.reshape(ND, P, -1, P).transpose(2, 1, 0, 3).reshape(-1, P, UNIT)

    def wide(w):
        return w.reshape(4, 2, P, 512).transpose(0, 2, 1, 3).reshape(4, P, UNIT)

    def ffn_units(l, n):
        units, f0 = [], 0
        gate, up = columns(wg[l, n]), columns(wu[l, n])
        for size in PARTS:
            units.append(np.stack([gate[f0:f0 + size], up[f0:f0 + size]], 1).reshape(2 * size, P, UNIT))
            down = np.zeros((ND, P, 8, P), np.float32)
            down[:, :, :size] = wd[l, n][f0 * P:(f0 + size) * P].reshape(size, P, ND, P).transpose(2, 1, 0, 3)
            units.append(down.reshape(ND, P, UNIT))
            f0 += size
        return units

    def mixer_units(l):
        w = w_in[l]
        wq, wzf, wzb, wi, wgt, wpv = (w[:, 512 * n:512 * (n + 1)] for n in range(6))
        wga, wgb = columns(w[:, 3072:4096]), columns(w[:, 4096:5120])
        heads = np.stack([columns(m) for m in (wq, wzf, wzb, wgt)], 1)
        units = [wide(wi), heads[0]]
        for n in range(NH - 1):
            units += [heads[n + 1], wga[2 * n:2 * n + 2]]
        units += [wga[6:8], wide(wpv)]
        branch = np.stack([m.reshape(4, P, ND, P).transpose(2, 1, 0, 3) for m in (wa[l], wb[l])], 2)
        units.append(np.stack([wgb, branch.reshape(ND, P, UNIT)], 1).reshape(2 * ND, P, UNIT))
        units.append(columns(w_out[l]))
        return units

    start = columns(ada_w[0][:, :START * P])
    weights = np.concatenate([start] + [u for l in range(NLAYER) for u in ffn_units(l, 0) + mixer_units(l) + ffn_units(l, 1)])
    assert weights.shape == (N_UNITS, P, UNIT)
    adaw = np.ascontiguousarray(ada_w.transpose(0, 2, 1)).reshape(-1, P, D)[START:]
    resid = np.concatenate([x[0], ctx[0]]).T.reshape(ND, P, ALL).transpose(1, 0, 2)
    cols = np.concatenate([norm_w.reshape(-1, P), ada_b.reshape(-1, P), hg_norm_w.reshape(-1, P),
                           pool_scale.reshape(-1, P), lower_bounds.reshape(-1, P), final_norm_w.reshape(-1, P)]).T
    assert cols.shape == (P, N_COLS)

    def box_1d(n, w):
        m = np.zeros((n, n), np.float64)
        for i in range(n):
            lo, hi = max(i - w // 2, 0), min(i + w - w // 2, n)
            m[i, lo:hi] = 1.0 / (hi - lo)
        return m

    box = np.zeros((2, P, 2, NG, TOK), np.float32)
    for g, w in enumerate(WINDOWS):
        grid = np.kron(box_1d(TOK // GRID_W, w), box_1d(GRID_W, w))
        for s, m in enumerate((grid, box_1d(TOK, w))):
            box[s, :, :, g, :] = (m - np.eye(TOK)).T.reshape(2, P, TOK).transpose(1, 0, 2)
    i = np.arange(P)
    masks = np.stack([((i[:, None] >> (n + 1)) == (i[None] >> (n + 1))) & ((i[:, None] >> n) != (i[None] >> n))
                      for n in range(NLEVEL)], 1).astype(np.float32)

    arrays = {
        "resid": resid, "c": np.stack([c[0], c_ctx]),
        "c_cols": np.stack([c[0], c_ctx]).reshape(2, ND, P).transpose(2, 1, 0), "cols": cols,
        "poolw": pool_w.transpose(0, 2, 1, 3), "box": box, "masks": masks,
        "ident": np.eye(P, dtype=np.float32), "weights": weights, "adaw": adaw,
    }
    nc = bacc.Bacc("TRN2", target_bir_lowering=False, num_devices=1)
    args = []
    for name, a in arrays.items():
        arrays[name] = a = np.ascontiguousarray(a)
        args.append(nc.dram_tensor(name, a.shape, mybir.dt.from_np(a.dtype), kind="ExternalInput").ap())
    out = nc.dram_tensor("out", (P, ND, TOK), F32, kind="ExternalOutput").ap()
    program(nc, *args, out)
    got = run_bass_kernel_spmd(nc, [arrays], core_ids=[0]).results[0]["out"]
    return np.ascontiguousarray(got.transpose(2, 1, 0).reshape(1, TOK, D))
```

```python
from contextlib import ExitStack

import numpy as np

import concourse.bass as bass
import concourse.mybir as mybir
from concourse.alu_op_type import AluOpType as ALU

ACT = mybir.ActivationFunctionType
F32 = mybir.dt.float32
F32R = mybir.dt.float32r
BF16 = mybir.dt.bfloat16
U8 = mybir.dt.uint8

P = 128
D = 1024
ND = D // P
TOK = 256
ALL = 2 * TOK
NLAYER = 2
NMOD = 9
NF = 2816 // P
PARTS = (8, 8, 6)
NH = 4
NG = 4
WINDOWS = (2, 4, 8, 16)
GRID_W = 64
EPS = 1e-6
UNIT = 1024
RING = 4
AHEAD = 3
START = 2 * ND
NLEVEL = 7
STEP_CROSS, STEP_STATE = NLEVEL + 1, NLEVEL + 2
NSTEP = NLEVEL + 3
OUT_BANK = (3, 0, 1, 2)

FFN_UNITS = 2 * NF + len(PARTS) * ND
MIX_UNITS = 4 + 4 + 3 * 6 + 6 + 2 * ND + ND
LAYER_UNITS = 2 * FFN_UNITS + MIX_UNITS
N_UNITS = START + NLAYER * LAYER_UNITS
FFN_ADA = NF + 2 * ND
N_ADA = NLAYER * NMOD * ND - START

C_NORM = 0
C_ADAB = C_NORM + NLAYER * 3 * ND
C_HGW = C_ADAB + NLAYER * NMOD * ND
C_PSC = C_HGW + NLAYER * NH
C_LB = C_PSC + NLAYER * NG
C_FIN = C_LB + 2 * NLAYER * NH
N_COLS = C_FIN + ND


def ffn_base(layer, which):
    return START + layer * LAYER_UNITS + which * (FFN_UNITS + MIX_UNITS)


def mix_base(layer):
    return START + layer * LAYER_UNITS + FFN_UNITS


def ada_plan():
    plan, at = {}, 0
    for key, n in (((0, "ffn0"), FFN_ADA), ((0, "mix"), ND + 4), ((0, "ffn1"), FFN_ADA),
                   ((1, "ffn0"), FFN_ADA), ((1, "mix"), 2)):
        plan[key] = (at, n)
        at += n
    assert at == N_ADA
    return plan


ADA = ada_plan()


def program(nc, resid_in, c_in, c_cols_in, cols_in, poolw_in, box_in, masks_in, ident_in, weights, adaw, out):
    with ExitStack() as stack:
        sem = lambda name: stack.enter_context(nc.semaphore(name))

        at = [16640]

        def sb(name, shape, dt=F32, where=None):
            size = int(np.prod(shape[1:])) * mybir.dt.size(dt)
            offset = at[0] if where is None else where
            if where is None:
                at[0] += (size + 31) // 32 * 32
            return nc.alloc_sbuf_tensor_at(name, list(shape), dt, offset=offset), offset

        raw, raw_at = sb("raw", [P, RING, UNIT])
        w_lo, _ = sb("w_lo", [P, RING, ND, P], F32R, raw_at)
        w_hi, _ = sb("w_hi", [P, RING, ND, P], F32R)
        ada_raw, _ = sb("ada_raw", [P, 2, D])
        silu_c, _ = sb("silu_c", [P, 2, D])
        junk, _ = sb("junk", [P, 2, D], BF16)
        u_hi, u_hi_at = sb("u_hi", [P, ND, ALL], F32R)
        u_lo, _ = sb("u_lo", [P, ND, ALL], F32R)
        h, _ = sb("h", [P, ND, ALL])
        hid_hi, hid_hi_at = sb("hid_hi", [P, 8, ALL], F32R)
        hid_lo, hid_lo_at = sb("hid_lo", [P, 8, ALL], F32R)
        a_hi, a_lo = hid_hi[:, 0:4, :], hid_lo[:, 0:4, :]
        p_hi, p_lo = hid_hi[:, 4:8, :], hid_lo[:, 4:8, :]
        box = [sb(f"box{s}", [P, 2, NG, TOK], F32, at_)[0]
               for s, at_ in enumerate((hid_hi_at + 8192, hid_lo_at + 8192))]
        mixed, _ = sb("mixed", [P, 2, 2, ALL], F32, hid_hi_at + 8192)
        S, T, A, AX, scan_at = [], [], [], [], []
        for par in range(2):
            t, where = sb(f"S{par}", [P, 4, ALL])
            scan_at.append(where)
            S.append(t)
            T.append(sb(f"T{par}", [P, 2, ALL])[0])
            A.append(sb(f"A{par}", [P, 2, 2 * TOK])[0])
            AX.append(sb(f"AX{par}", [P, 2, TOK])[0])
        v, v_at = sb("v", [P, 4, NH * P])
        masks_f, _ = sb("masks_f", [P, NLEVEL, P], F32, v_at)
        gs, _ = sb("gs", [P, 2, ALL])
        sig_a, sig_a_at = sb("sig_a", [P, ND, ALL])
        m_hi, _ = sb("m_hi", [P, ND, ALL], F32R, scan_at[0])
        m_lo, _ = sb("m_lo", [P, ND, ALL], F32R, sig_a_at)
        silu_t, _ = sb("silu_t", [P, 2, ALL], F32, scan_at[0])
        hid_t, _ = sb("hid_t", [P, 2, ALL], F32, scan_at[0] + 4096)
        pv, _ = sb("pv", [P, 4, NG * P], F32, scan_at[0])
        dpool, _ = sb("dpool", [P, NG, ALL], F32, scan_at[0] + 8192)
        sq, _ = sb("sq", [P, 2, ALL], F32, scan_at[1])
        sq_sum, _ = sb("sq_sum", [P, ALL], F32, scan_at[1] + 4096)
        diag, _ = sb("diag", [P, ALL // P, P], F32, scan_at[1] + 6144)
        norm_t, _ = sb("norm_t", [P, 4, ALL], F32, scan_at[1] + 8192)
        sig_b, _ = sb("sig_b", [P, 2, ALL], F32, scan_at[1])
        mix_t, _ = sb("mix_t", [P, 2, 2, ALL], F32, scan_at[1] + 4096)
        start_w = [sb(f"start_w{n}", [P, START // 2, UNIT], F32, at_)[0] for n, at_ in enumerate((u_hi_at, hid_hi_at))]
        start_rows, _ = sb("start_rows", [P, 4, 512], F32, scan_at[1] + 8192)
        head_t, _ = sb("head_t", [P, 2, ALL])
        r_cols, _ = sb("r_cols", [P, 2, ALL // P])
        c_cols, _ = sb("c_cols", [P, ND, 2])
        cols, _ = sb("cols", [P, N_COLS])
        mod, _ = sb("mod", [P, 2, NLAYER * NMOD * ND])
        scale_c, _ = sb("scale_c", [P, 2, ND])
        shift_c, _ = sb("shift_c", [P, 2, ND])
        gate_c, _ = sb("gate_c", [P, 2, ND])
        lb_e, _ = sb("lb_e", [P, 4, NLAYER * 2 * NH])
        lb, _ = sb("lb", [P, 2, NLAYER, NH])
        one_lb, _ = sb("one_lb", [P, 2, NLAYER, NH])
        masks, _ = sb("masks", [P, NLEVEL, P], U8)
        ident, _ = sb("ident", [P, P])
        ones, _ = sb("ones", [P, P])
        eps_c, _ = sb("eps_c", [P, 1])
        sqrt_junk, _ = sb("sqrt_junk", [P, 1])
        poolw, _ = sb("poolw", [P, NG, P])
        assert at[0] <= 229344, at[0]

        bank = [stack.enter_context(nc.psum_tensor(f"bank{i}", [P, 512], F32)) for i in range(8)]

        s_raw = [sem(f"raw_landed{i}") for i in range(RING)]
        s_start = [sem(f"start_chunk_landed{k}") for k in range(ND)]
        s_hi = sem("hi_ready")
        s_lo = sem("lo_ready")
        s_used = sem("units_multiplied")
        s_aland = [sem(f"ada_landed{i}") for i in range(2)]
        s_ada = sem("ada_done")
        s_load = sem("start_landed")
        s_hland = sem("residual_landed")
        s_mland = sem("masks_landed")
        s_cland = sem("c_landed")
        s_ccland = sem("c_columns_landed")
        s_const = sem("ones_written")
        s_silu_c = sem("silu_c_ready")
        s_rows = sem("start_rows_out")
        s_cols = sem("start_columns")
        s_up_free = sem("up_banks_free")
        s_silu = sem("silu_ready")
        s_hid_hi = sem("hid_hi_ready")
        s_hid_lo = sem("hid_lo_ready")
        s_res = sem("residual_added")
        s_sq = sem("squared")
        s_sqs = sem("squares_summed")
        s_ssq = sem("norm_total")
        s_table = sem("sqrt_table_loaded")
        s_std = sem("std_ready")
        s_diag = sem("diag_ready")
        s_bc = sem("rstd_spread")
        s_nt = sem("normed")
        s_uhi = sem("u_hi_ready")
        s_ulo = sem("u_lo_ready")
        s_chain = sem("vector_chain")
        s_proj = sem("projection_out")
        s_vout = sem("v_out")
        s_sga = sem("sig_a_out")
        s_prep = sem("operands_ready")
        s_mix = sem("directions_mixed")
        s_score = sem("scored")
        s_merge = sem("merged")
        s_cross = sem("cross_copied")
        s_av = sem("head_out")
        s_hsq = sem("head_squared")
        s_x1 = sem("head_weighted")
        s_hss = sem("head_total")
        s_hstd = sem("head_std")
        s_hdg = sem("head_diag")
        s_hbc = sem("head_rstd")
        s_at = sem("head_gated")
        s_ahi = sem("a_hi_ready")
        s_head = sem("head_done")
        s_pvo = sem("pv_out")
        s_box = sem("box_landed")
        s_dmm = sem("box_means")
        s_dout = sem("box_out")
        s_pmm = sem("pool_products")
        s_phi = sem("p_hi_ready")
        s_plo = sem("p_lo_ready")
        s_sgb = sem("sig_b_out")
        s_mt = sem("merge_a")
        s_mg = sem("branches_merged")
        s_fin = sem("out_rows")
        s_out = sem("out_stored")

        def view(t, offset, *dims):
            whole = t[:]
            return bass.AP(whole.tensor, offset, [[whole.ap[0][0], P]] + [list(x) for x in dims])

        def streams(ntok):
            return range(ntok // TOK)

        def span(s):
            return slice(s * TOK, (s + 1) * TOK)

        block = stack.enter_context(nc.Block())

        @block.sync
        def _(sp):
            sp.dma_start(c_cols[:], c_cols_in).then_inc(s_ccland, 16)
            for k in range(ND):
                sp.dma_start(start_w[k // 4][:, 2 * (k % 4):2 * (k % 4) + 2, :],
                             weights[2 * k:2 * k + 2].rearrange("a p n -> p a n")).then_inc(s_start[k], 16)
                if k == ND // 2 + 1:
                    sp.dma_start(h[:], resid_in).then_inc(s_hland, 16)
            for u in range(RING):
                sp.dma_start(raw[:, u, :], weights[START + u]).then_inc(s_raw[u], 16)
            with sp.Fori(START // RING + 1, N_UNITS // RING) as i:
                for j in range(RING):
                    sp.wait_ge(s_used, i * RING + (j - RING + 1))
                    sp.dma_start(raw[:, j, :], weights[bass.ds(i * RING + j, 1)].rearrange("a p n -> (a p) n")
                                 ).then_inc(s_raw[j], 16)
            for d in range(ND):
                sp.wait_ge(s_fin, d + 1)
                sp.dma_start(out[:, d, :], sig_a[:, d, 0:TOK]).then_inc(s_out, 16)
            sp.wait_ge(s_out, 16 * ND)

        @block.gpsimd
        def _(pool):
            pool.memset(ones[:], 1.0).then_inc(s_const, 1)
            pool.memset(eps_c[:], EPS).then_inc(s_const, 1)
            pool.wait_ge(s_diag, 1)
            pool.dma_start(silu_c[:], c_in.partition_broadcast(P)).then_inc(s_cland, 16)
            for n in range(2):
                pool.dma_start(ada_raw[:, n, :], adaw[n]).then_inc(s_aland[n], 16)
            pool.dma_start(masks_f[:], masks_in).then_inc(s_mland, 16)

            def load(first, count):
                with pool.Fori(first // 2, (first + count) // 2) as i:
                    for j in range(2):
                        pool.wait_ge(s_ada, i * 4 + 2 * j)
                        pool.dma_start(ada_raw[:, j, :], adaw[bass.ds(i * 2 + j, 1)].rearrange("a p n -> (a p) n")
                                       ).then_inc(s_aland[j], 16)

            def mixer_tables(layer):
                pool.wait_ge(s_score, NSTEP * (layer * NH + NH - 1) + NLEVEL + 1)
                for s in range(2):
                    pool.dma_start(box[s][:], box_in[s]).then_inc(s_box, 16)
                pool.dma_start(poolw[:], poolw_in[layer]).then_inc(s_box, 16)

            ahead = ADA[(0, "mix")][0] + 6
            load(2, ahead - 2)
            mixer_tables(0)
            load(ahead, N_ADA - ahead)
            mixer_tables(1)

        @block.tensor
        def _(pe):
            def half(ps, slot, k0, k1, hi, lo, unit_wait, chunk_wait=None, done=False, start=None, stop=None):
                if unit_wait is not None:
                    pe.wait_ge(s_lo, unit_wait - START)
                for k in range(k0, k1):
                    if chunk_wait is not None:
                        pe.wait_ge(chunk_wait[0], chunk_wait[1] + k + 1)
                    first = k == k0 if start is None else start and k == k0
                    last = k == k1 - 1 if stop is None else stop and k == k1 - 1
                    pe.matmul(ps, w_hi[:, slot, k, :], hi(k), start=first, stop=False)
                    pe.matmul(ps, w_hi[:, slot, k, :], lo(k), start=False, stop=False)
                    mm = pe.matmul(ps, w_lo[:, slot, k, :], hi(k), start=False, stop=last)
                if done:
                    mm.then_inc(s_used, 1)

            def totals(ps, squares, nt):
                for t in range(nt // P):
                    mm = pe.matmul(ps[:, t:t + 1], squares[:, t * P:(t + 1) * P], ones[:, 0:1],
                                   start=True, stop=True)
                return mm

            def start_columns():
                pe.wait_ge(s_load, 32)
                for b in range(START):
                    if b % 4 == 0:
                        pe.wait_ge(s_rows, b // 4 + 1)
                    mm = pe.matmul(bank[6][:, 2 * b:2 * b + 2], start_rows[0:2, b // 4, b % 4 * P:(b % 4 + 1) * P],
                                   ident[0:2, 0:2], start=True, stop=True)
                mm.then_inc(s_cols, 1)

            def norm_total(n):
                nt = norm_tok(n)
                pe.wait_ge(s_sqs, (ND + 1) * (n + 1))
                totals(bank[4], sq_sum, nt).then_inc(s_ssq, 1)
                if n == 0:
                    start_columns()
                pe.wait_ge(s_diag, n + 1)
                pe.matmul(bank[5][:, 0:nt], ones[:], view(diag, 0, [1, nt]), start=True, stop=True).then_inc(s_bc, 1)

            def pair(ps, slots, hi, lo, unit, chunk_wait):
                for g in range(2):
                    pe.wait_ge(s_lo, unit - START + g)
                for k in range(ND):
                    if chunk_wait is not None:
                        pe.wait_ge(chunk_wait[0], chunk_wait[1] + k + 1)
                    for p_, slot in zip(ps, slots):
                        pe.matmul(p_, w_hi[:, slot, k, :], hi(k), start=(k == 0), stop=False)
                        pe.matmul(p_, w_hi[:, slot, k, :], lo(k), start=False, stop=False)
                        mm = pe.matmul(p_, w_lo[:, slot, k, :], hi(k), start=False, stop=(k == ND - 1))
                        if k == ND - 1:
                            mm.then_inc(s_used, 1)

            def ffn(layer, which, n_norm):
                ntok = ffn_tok(layer, which)
                hi, lo = (lambda k: u_hi[:, k, 0:ntok]), (lambda k: u_lo[:, k, 0:ntok])
                hh, hl = (lambda k: hid_hi[:, k, 0:ntok]), (lambda k: hid_lo[:, k, 0:ntok])
                norm_total(n_norm)
                base = ffn_base(layer, which)
                hid, res = hid_count(layer, which), res_count(layer, which)

                def up(i, b):
                    pe.wait_ge(s_up_free, i * 2 + (hid + b + 1))
                    for j in (2 * b, 2 * b + 1):
                        half(bank[j][:, 0:ntok], j, 0, ND, hi, lo, i * 4 + (base + j + 1), done=True)

                for part, n in enumerate(PARTS):
                    if part == 0:
                        pe.wait_ge(s_up_free, hid + 1)
                        pair((bank[0][:, 0:ntok], bank[1][:, 0:ntok]), (0, 1), hi, lo, base + 1,
                             (s_ulo, u_count(n_norm)))
                        up(0, 1)
                    with pe.Fori(int(part == 0), n // 2) as i:
                        up(i, 0)
                        up(i, 1)
                    base += 2 * n
                    with pe.Fori(0, ND // 4) as i:
                        for j in range(4):
                            pe.wait_ge(s_res, i * 4 + (res + j + 1))
                            half(bank[4 + j][:, 0:ntok], j % RING, 0, n, hh, hl, i * 4 + (base + j + 1),
                                 (s_hid_lo, hid) if j == 0 else None, done=True)
                    base += ND
                    hid += n
                    res += ND

            def scan_step(layer, head, step):
                n = layer * NH + head
                Sh = S[head % 2]
                ps = bank[6 if step == STEP_STATE else 4 + step % 2]
                pe.wait_ge(s_prep, NSTEP * n + step + 1)
                if 1 <= step <= NLEVEL:
                    pe.wait_ge(s_mix, NLEVEL * n + step)
                tiles = range(2 * (ffn_tok(layer, 1) // TOK))
                if step == STEP_STATE:
                    for a in range(2):
                        k0 = TOK + a * P
                        pe.matmul(ps[:, a * TOK:(a + 1) * TOK], Sh[:, 0, k0:k0 + P], Sh[:, 2, 0:TOK],
                                  start=True, stop=False)
                        mm = pe.matmul(ps[:, a * TOK:(a + 1) * TOK], Sh[:, 3, k0:k0 + P], Sh[:, 1, 0:TOK],
                                       start=False, stop=True)
                elif step == STEP_CROSS:
                    for t in tiles:
                        here, there = t * P, (t ^ 1) * P
                        key, query = (0, 2) if t % 2 == 0 else (3, 1)
                        mm = pe.matmul(ps[:, here:here + P], Sh[:, key, here:here + P],
                                       Sh[:, query, there:there + P], start=True, stop=True)
                else:
                    for t in tiles:
                        if step == 0:
                            mm = pe.matmul(ps[:, t * P:(t + 1) * P], Sh[:, 2, t * P:(t + 1) * P],
                                           Sh[:, 1, t * P:(t + 1) * P], start=True, stop=True)
                            continue
                        here = slice(t * P, (t + 1) * P)
                        mm = pe.matmul(ps[:, here], mixed[:, step % 2, 0, here], mixed[:, step % 2, 1, here],
                                       start=True, stop=True)
                mm.then_inc(s_score, 1)

            def head_out(layer, head):
                n = layer * NH + head
                par = head % 2
                vh = lambda tile: v[:, tile, head * P:(head + 1) * P]
                pe.wait_ge(s_merge, (NLEVEL + 1) * (n + 1))
                pe.wait_ge(s_cross, 2 * (n + 1))
                pe.wait_ge(s_proj, 6 * (n + 1))
                o = bank[7]
                for a in range(2):
                    pe.matmul(o[:, 0:TOK], vh(a), A[par][:, 0, a * TOK:(a + 1) * TOK], start=(a == 0), stop=False)
                for a in range(2):
                    mm = pe.matmul(o[:, 0:TOK], vh(2 + a), AX[par][:, a, :], start=False, stop=(a == 1))
                if ffn_tok(layer, 1) == ALL:
                    for a in range(2):
                        mm = pe.matmul(o[:, TOK:ALL], vh(2 + a), A[par][:, 1, a * TOK:(a + 1) * TOK],
                                       start=(a == 0), stop=(a == 1))
                mm.then_inc(s_av, 1)

            def head_total(layer, head):
                n = layer * NH + head
                pe.wait_ge(s_hsq, n + 1)
                totals(bank[6], head_t[:, 0, :], ffn_tok(layer, 1)).then_inc(s_hss, 1)

            def head_spread(layer, head):
                n = layer * NH + head
                nt = ffn_tok(layer, 1)
                pe.wait_ge(s_hdg, n + 1)
                pe.matmul(bank[6][:, 0:nt], ones[:], head_t[:, 0, 0:nt], start=True, stop=True).then_inc(s_hbc, 1)

            def natural(ps0, unit, j, ntile, half_of=(0, 2), u_wait=None):
                slot = unit % RING
                if half_of[0] == 0:
                    pe.wait_ge(s_lo, unit + 1 - START)
                for kk in range(*half_of):
                    k = 2 * j + kk
                    if u_wait is not None:
                        pe.wait_ge(s_ulo, u_wait + k + 1)
                    wh = view(w_hi, slot * UNIT + kk * 512, [1, 512])
                    wl = view(w_lo, slot * UNIT + kk * 512, [1, 512])
                    for t in range(ntile):
                        ts = slice(t * P, (t + 1) * P)
                        pe.matmul(bank[ps0 + t][:], u_hi[:, k, ts], wh, start=(k == 0), stop=False)
                        pe.matmul(bank[ps0 + t][:], u_hi[:, k, ts], wl, start=False, stop=False)
                        mm = pe.matmul(bank[ps0 + t][:], u_lo[:, k, ts], wh, start=False, stop=(k == ND - 1))
                if half_of[1] == 2:
                    mm.then_inc(s_used, 1)

            def mixer(layer, n_norm):
                nt = ffn_tok(layer, 1)
                ntile = nt // P
                hi = lambda m: (lambda k: u_hi[:, k, 0:m])
                lo = lambda m: (lambda k: u_lo[:, k, 0:m])
                unit = mix_base(layer)
                n0 = layer * NH
                norm_total(n_norm)
                pe.wait_ge(s_res, res_count(layer, 0) + 4 + 3 * ND)
                for j in range(4):
                    natural(0, unit + j, j, 4, u_wait=u_count(n_norm))
                unit += 4
                for j in range(4):
                    m = nt if j in (0, 3) else ALL
                    half(bank[4 + j][:, 0:m], j % RING, 0, ND, hi(m), lo(m), unit + j + 1, done=True)
                unit += 4
                for head in range(NH):
                    n = n0 + head
                    for piece in range(12):
                        j, second = piece // 2, piece % 2
                        k0 = 4 * second
                        if head < NH - 1 or j < 2:
                            if head < NH - 1:
                                m = nt if j in (0, 3, 4, 5) else ALL
                                b = j % 4
                            else:
                                m, b = nt, j
                            if not second:
                                if head == 0 and j == 0:
                                    pe.wait_ge(s_vout, layer + 1)
                                elif head < NH - 1 and j in (0, 1):
                                    pe.wait_ge(s_sga, layer * ND + 2 * head - 1 + j)
                                elif head < NH - 1 and j in (2, 3):
                                    pe.wait_ge(s_proj, 6 * (n + 1))
                                elif head < NH - 1 and j == 4:
                                    pe.wait_ge(s_proj, 6 * (n + 1) + 1)
                                elif head < NH - 1 and j == 5:
                                    pe.wait_ge(s_proj, 6 * (n + 1) + 3)
                                else:
                                    pe.wait_ge(s_proj, 6 * (n + 1))
                                    pe.wait_ge(s_sga, layer * ND + 2 * head - 1 + j)
                            half(bank[b][:, 0:m], (unit + j) % RING, k0, k0 + 4, hi(m), lo(m),
                                 unit + j + 1 if not second else None, done=bool(second),
                                 start=not second, stop=bool(second))
                        else:
                            if j == 2 and not second:
                                pe.wait_ge(s_sga, layer * ND + ND)
                            natural(0, unit + j, j - 2, ntile, (second, second + 1))
                        if piece < NSTEP:
                            scan_step(layer, head, piece)
                            if piece == 1 and head:
                                head_spread(layer, head - 1)
                        elif piece == NSTEP:
                            head_out(layer, head)
                        else:
                            head_total(layer, head)
                    unit += 6
                pe.wait_ge(s_box, 48 * (layer + 1))
                pe.wait_ge(s_pvo, 2 * (layer + 1))
                for g in range(NG):
                    for s in streams(nt):
                        for a in range(2):
                            mm = pe.matmul(bank[g][:, span(s)], pv[:, 2 * s + a, g * P:(g + 1) * P],
                                           box[s][:, a, g, :], start=(a == 0), stop=(a == 1))
                    mm.then_inc(s_dmm, 1)
                head_spread(layer, NH - 1)
                pe.wait_ge(s_head, n0 + NH)
                for g in range(NG):
                    pe.wait_ge(s_dout, layer * NG + g + 1)
                    pe.matmul(bank[4 + g][:, 0:nt], poolw[:, g, :], dpool[:, g, 0:nt],
                              start=True, stop=True).then_inc(s_pmm, 1)
                with pe.Fori(0, ND // 2) as i:
                    for b in range(2):
                        pe.wait_ge(s_mg, i * 2 + (layer * ND + b + 1))
                        half(bank[4 * b][:, 0:nt], 2 * b, 0, ND, hi(nt), lo(nt), i * 4 + (unit + 2 * b + 1), done=True)
                        if b == 0:
                            pe.wait_ge(s_plo, (layer + 1) * NG)
                        half(bank[4 * b + 1][:, 0:nt], 2 * b + 1, 0, 4, lambda k: a_hi[:, k, 0:nt],
                             lambda k: a_lo[:, k, 0:nt], i * 4 + (unit + 2 * b + 2))
                        half(bank[4 * b + 2][:, 0:nt], 2 * b + 1, 4, 8, lambda k: p_hi[:, k - 4, 0:nt],
                             lambda k: p_lo[:, k - 4, 0:nt], None, done=True)
                unit += 2 * ND
                res = res_count(layer, 0) + 3 * ND
                with pe.Fori(0, ND // 4) as i:
                    for j in range(4):
                        if j == 0:
                            pe.wait_ge(s_mg, layer * ND + ND + 1)
                        pe.wait_ge(s_res, i * 4 + (res + j + 1))
                        half(bank[OUT_BANK[j]][:, 0:nt], j % RING, 0, ND, lambda k: m_hi[:, k, 0:nt],
                             lambda k: m_lo[:, k, 0:nt], i * 4 + (unit + j + 1),
                             (s_ulo, u_count(n_norm) + ND) if j == 0 else None, done=True)

            pe.wait_ge(s_silu_c, 1)
            for u in range(START):
                k, m = u // 2, u % 2
                if m == 0:
                    pe.wait_ge(s_start[k], 16)
                for q in range(2):
                    mm = pe.matmul(bank[2 * m + q][0:2, :], c_cols[:, k, :],
                                   start_w[k // 4][:, u % ND, q * 512:(q + 1) * 512],
                                   start=(k == 0), stop=(k == ND - 1))
                mm.then_inc(s_used, 1)
            pe.wait_ge(s_const, 2)
            n_norm = 0
            for layer in range(NLAYER):
                ffn(layer, 0, n_norm)
                mixer(layer, n_norm + 1)
                ffn(layer, 1, n_norm + 2)
                n_norm += 3
            norm_total(n_norm)

        @block.scalar
        def _(act):
            tables = [0]

            def split_next(base, i, j):
                act.wait_ge(s_used, i * 4 + (base + j - RING + 1) if i is not None else base + j - RING + 1)
                landed = (base + j - START) // RING + 1
                act.wait_ge(s_raw[j % RING], ((i + landed) if i is not None else landed) * 16)
                act.activation(view(w_hi, (j % RING) * UNIT, [1, UNIT]), raw[:, j % RING, :], ACT.Copy
                               ).then_inc(s_hi, 1)

            def square(n, i, d, res):
                nt = norm_tok(n)
                at4 = (lambda x: i * 4 + x) if i is not None else (lambda x: x)
                act.wait_ge(s_res, at4(4 + res + d + 1))
                if n or d:
                    act.wait_ge(s_sqs, at4((ND + 1) * n + d))
                src = h[:, bass.ds(at4(d), 1), 0:nt].rearrange("p a n -> p (a n)")
                act.activation(sq[:, d % 2, 0:nt], src, ACT.Square).then_inc(s_sq, 1)

            def load_sqrt():
                tables[0] += 1
                act.activation(sqrt_junk[:], eps_c[:], ACT.Sqrt).then_inc(s_table, 1)
                act.wait_ge(s_table, tables[0])

            def norm(n, to_u=True):
                nt = norm_tok(n)
                act.wait_ge(s_ssq, n + 1)
                act.activation(r_cols[:, 0, 0:nt // P], bank[4][:, 0:nt // P], ACT.Sqrt, bias=eps_c[:], scale=1.0 / D
                               ).then_inc(s_std, 1)
                if not to_u:
                    return
                if n == 0:
                    for j in range(AHEAD - 1):
                        split_next(START, None, j)
                for d in range(ND):
                    for s in streams(nt):
                        act.wait_ge(s_nt, 2 * ND * n + 2 * d + (s + 1) * 2 * TOK // nt)
                        ins = act.activation(u_hi[:, d, span(s)], norm_t[:, d % 4, span(s)], ACT.Identity,
                                             bias=shift_c[:, s, d:d + 1])
                    ins.then_inc(s_uhi, 1)

            def ffn(layer, which, n_norm):
                nt = ffn_tok(layer, which)
                norm(n_norm)
                if n_norm == 0:
                    split_next(START, None, AHEAD - 1)
                    act.wait_ge(s_cland, 16)
                    act.activation(silu_c[:], silu_c[:], ACT.Silu).then_inc(s_silu_c, 1)
                base = ffn_base(layer, which)
                hid = hid_count(layer, which)
                last_ffn = layer == NLAYER - 1 and which == 1
                for part, n in enumerate(PARTS):
                    with act.Fori(0, n // 2) as i:
                        for b in range(2):
                            split_next(base, i, 2 * b + AHEAD)
                            act.wait_ge(s_used, i * 4 + (base + 2 * b + 2))
                            act.activation(silu_t[:, b, 0:nt], bank[2 * b][:, 0:nt], ACT.Silu).then_inc(s_silu, 1)
                            act.wait_ge(s_up_free, i * 2 + (hid + b + 3))
                            act.activation(hid_hi[:, bass.ds(i * 2 + b, 1), 0:nt].rearrange("p a n -> p (a n)"),
                                           hid_t[:, b, 0:nt], ACT.Copy).then_inc(s_hid_hi, 1)
                            split_next(base, i, 2 * b + AHEAD + 1)
                    base += 2 * n
                    hid += n
                    rounds = ND // 4
                    if last_ffn and part == len(PARTS) - 1:
                        rounds -= 1
                    to_norm = part == len(PARTS) - 1
                    res = res_count(layer, which) + part * ND
                    if to_norm:
                        load_sqrt()
                    with act.Fori(0, rounds) as i:
                        for j in range(4):
                            split_next(base, i, j + AHEAD)
                            if to_norm:
                                square(n_norm + 1, i, j, res)
                    if rounds < ND // 4:
                        split_next(base + 4 * rounds, None, AHEAD)
                        for j in range(4):
                            square(n_norm + 1, None, 4 * rounds + j, res)
                    base += ND

            def proj(layer, head, which, ps, nt):
                par = head % 2
                if which == 0:
                    if layer * NH + head >= 2:
                        act.wait_ge(s_x1, layer * NH + head - 1)
                    act.activation(S[par][:, 1, 0:nt], ps[:, 0:nt], ACT.Silu).then_inc(s_proj, 1)
                elif which == 3:
                    act.activation(gs[:, par, 0:nt], ps[:, 0:nt], ACT.Silu).then_inc(s_proj, 1)
                else:
                    act.activation(T[par][:, which - 1, :], ps[:], ACT.Sigmoid).then_inc(s_proj, 1)
                    act.activation(S[par][:, 0 if which == 1 else 3, :], ps[:], ACT.Sigmoid, scale=-1.0
                                   ).then_inc(s_proj, 1)

            def mix_directions(n, step, nt):
                act.wait_ge(s_prep, NSTEP * n + step + 1)
                act.wait_ge(s_score, NSTEP * n + step - 1)
                hb = 1 << (step - 1)
                for m, (array, other) in enumerate(((0, 3), (1, 2))):
                    ins = act.activation(view(mixed, (step % 2 * 2 + m) * ALL, [2 * hb, nt // (2 * hb)], [hb, 2], [1, hb]),
                                         view(S[n % 2], array * ALL, [2 * hb, nt // (2 * hb)],
                                              [(other - array) * ALL + hb, 2], [1, hb]), ACT.Copy)
                ins.then_inc(s_mix, 1)

            def head_std(n, nt):
                act.wait_ge(s_hss, n + 1)
                act.activation(r_cols[:, 1, 0:nt // P], bank[6][:, 0:nt // P], ACT.Sqrt, bias=eps_c[:],
                               scale=1.0 / P).then_inc(s_hstd, 1)

            def head_hi(layer, head, nt):
                act.wait_ge(s_at, layer * NH + head + 1)
                act.activation(a_hi[:, head, 0:nt], head_t[:, 1, 0:nt], ACT.Copy).then_inc(s_ahi, 1)

            def mixer(layer, n_norm):
                nt = ffn_tok(layer, 1)
                base = mix_base(layer)
                norm(n_norm)
                for j in range(4):
                    if j == 3:
                        split_next(base, None, j + AHEAD)
                        act.wait_ge(s_used, base + 4)
                        for t in range(4):
                            ins = act.activation(v[:, t, :], bank[t][:], ACT.Copy)
                        ins.then_inc(s_vout, 1)
                    else:
                        split_next(base, None, j + AHEAD)
                base += 4
                for j in range(4):
                    split_next(base, None, j + AHEAD)
                    act.wait_ge(s_used, base + j + 1)
                    proj(layer, 0, j, bank[4 + j], nt if j in (0, 3) else ALL)
                base += 4
                for head in range(NH):
                    n = layer * NH + head
                    par = head % 2
                    for piece in range(12):
                        j = piece // 2
                        if piece % 2:
                            split_next(base + j - (base + j) % 4, None, (base + j) % 4 + AHEAD)
                        if piece < NLEVEL:
                            mix_directions(n, piece + 1, nt)
                        if piece % 2:
                            act.wait_ge(s_used, base + j + 1)
                            if head < NH - 1:
                                if j < 4:
                                    proj(layer, head + 1, j, bank[j], nt if j in (0, 3) else ALL)
                                else:
                                    act.activation(sig_a[:, 2 * head + j - 4, 0:nt], bank[j - 4][:, 0:nt],
                                                   ACT.Sigmoid).then_inc(s_sga, 1)
                            elif j < 2:
                                act.activation(sig_a[:, 2 * head + j, 0:nt], bank[j][:, 0:nt], ACT.Sigmoid
                                               ).then_inc(s_sga, 1)
                        if piece == 2 and head:
                            head_hi(layer, head - 1, nt)
                        if piece == STEP_CROSS:
                            act.wait_ge(s_score, NSTEP * n + STEP_CROSS + 1)
                            for s in streams(nt):
                                ins = act.activation(A[par][:, s, P:3 * P], bank[4][:, span(s)], ACT.Copy)
                            ins.then_inc(s_cross, 1)
                        elif piece == STEP_STATE:
                            act.wait_ge(s_score, NSTEP * n + STEP_STATE + 1)
                            act.activation(AX[par][:], bank[6][:].rearrange("p (a t) -> p a t", a=2), ACT.Copy
                                           ).then_inc(s_cross, 1)
                        elif piece == NSTEP:
                            act.wait_ge(s_av, n + 1)
                            if n:
                                act.wait_ge(s_head, n)
                            act.activation(head_t[:, 0, 0:nt], bank[7][:, 0:nt], ACT.Square).then_inc(s_hsq, 1)
                        elif piece == NSTEP + 1:
                            head_std(n, nt)
                    base += 6
                for t in range(nt // P // 2):
                    ins = act.activation(pv[:, t, :], bank[t][:], ACT.Copy)
                ins.then_inc(s_pvo, 1)
                for g in range(NG):
                    act.wait_ge(s_dmm, layer * NG + g + 1)
                    act.activation(dpool[:, g, 0:nt], bank[g][:, 0:nt], ACT.Copy).then_inc(s_dout, 1)
                head_hi(layer, NH - 1, nt)
                psc = lambda g: cols[:, C_PSC + layer * NG + g:C_PSC + layer * NG + g + 1]
                for g in range(NG):
                    act.wait_ge(s_pmm, layer * NG + g + 1)
                    act.activation(p_hi[:, g, 0:nt], bank[4 + g][:, 0:nt], ACT.Copy, scale=psc(g)).then_inc(s_phi, 1)

                def merged_hi(d):
                    act.wait_ge(s_mg, d + (layer * ND + 3))
                    act.activation(m_hi[:, bass.ds(d, 1), 0:nt].rearrange("p a n -> p (a n)"),
                                   sig_a[:, bass.ds(d, 1), 0:nt].rearrange("p a n -> p (a n)"), ACT.Copy
                                   ).then_inc(s_uhi, 1)

                def gate_b(i, b, before):
                    split_next(base, i, 2 * b + AHEAD)
                    act.wait_ge(s_used, i * 4 + (base + 2 * b + 1))
                    act.wait_ge(s_mg, i * 2 + (layer * ND + b + 1))
                    act.activation(sig_b[:, b, 0:nt], bank[4 * b][:, 0:nt], ACT.Sigmoid).then_inc(s_sgb, 1)
                    if before is not None:
                        merged_hi(before)
                    split_next(base, i, 2 * b + AHEAD + 1)

                gate_b(0, 0, None)
                gate_b(0, 1, 0)
                with act.Fori(1, ND // 2) as i:
                    gate_b(i, 0, i * 2 - 1)
                    gate_b(i, 1, i * 2)
                merged_hi(ND - 1)
                base += 2 * ND
                load_sqrt()
                with act.Fori(0, ND // 4) as i:
                    for j in range(4):
                        split_next(base, i, j + AHEAD)
                        square(n_norm + 1, i, j, res_count(layer, 0) + len(PARTS) * ND)

            act.dma_start(cols[:], cols_in).then_inc(s_load, 16)
            act.dma_start(ident[:], ident_in).then_inc(s_load, 16)
            act.wait_ge(s_ccland, 16)
            act.activation(c_cols[:], c_cols[:], ACT.Silu).then_inc(s_silu_c, 1)
            act.wait_ge(s_chain, 1 + NLAYER)
            act.activation(lb_e[:, 1, :], lb_e[:, 0, :], ACT.Exp).then_inc(s_silu_c, 1)
            act.wait_ge(s_hland, 16)
            for d in range(ND):
                square(0, None, d, -d - 1)
            act.wait_ge(s_const, 2)
            n_norm = 0
            for layer in range(NLAYER):
                ffn(layer, 0, n_norm)
                mixer(layer, n_norm + 1)
                ffn(layer, 1, n_norm + 2)
                n_norm += 3
            norm(n_norm, to_u=False)

        @block.vector
        def _(dve):
            chain = [0]

            def link(ins):
                chain[0] += 1
                ins.then_inc(s_chain, 1)
                dve.wait_ge(s_chain, chain[0])

            def split_lo(base, i, j):
                dve.wait_ge(s_hi, i * 4 + (base + j + 1 - START) if i is not None else base + j + 1 - START)
                dve.tensor_tensor(view(w_lo, (j % RING) * UNIT, [1, UNIT]), raw[:, j % RING, :],
                                  view(w_hi, (j % RING) * UNIT, [1, UNIT]).bitcast(F32), ALU.subtract
                                  ).then_inc(s_lo, 1)

            def ada_pair(pair, first):
                for j in range(2):
                    dve.wait_ge(s_aland[j], (pair + first // 2 + 1) * 16)
                    for s in range(2):
                        dve.wait_ge(s_ada, pair * 4 + (2 * (first + j) + s + 1))
                        dve.scalar_tensor_tensor(
                            out=junk[:, s, :], in0=ada_raw[:, j, :], scalar=1.0, in1=silu_c[:, s, :],
                            op0=ALU.mult, op1=ALU.mult,
                            accum_out=mod[:, s, bass.ds(pair * 2 + (START + first + j), 1)]).then_inc(s_ada, 1)

            def column(t, k, layer):
                return view(cols, C_ADAB + (layer * NMOD + k) * ND, [0, 2], [1, ND])

            def mod_of(layer, k):
                at0 = (layer * NMOD + k) * ND
                return mod[:, :, at0:at0 + ND]

            def norm_columns(layer, k0, norm_i):
                if layer or k0:
                    dve.wait_ge(s_ada, 2 + 2 * ((layer * NMOD + k0 + 2) * ND - START))
                link(dve.tensor_tensor(scale_c[:], mod_of(layer, k0 + 1), column(cols, k0 + 1, layer), ALU.add))
                link(dve.scalar_tensor_tensor(out=scale_c[:], in0=scale_c[:], scalar=1.0,
                                              in1=view(cols, C_NORM + (layer * 3 + norm_i) * ND, [0, 2], [1, ND]),
                                              op0=ALU.add, op1=ALU.mult))
                link(dve.tensor_tensor(shift_c[:], mod_of(layer, k0), column(cols, k0, layer), ALU.add))

            def gate_columns(layer, k, factor):
                dve.wait_ge(s_ada, 2 + 2 * ((layer * NMOD + k + 1) * ND - START))
                link(dve.tensor_tensor(gate_c[:], mod_of(layer, k), column(cols, k, layer), ALU.add))
                link(dve.tensor_scalar(gate_c[:], gate_c[:], factor, None, ALU.mult))

            def spread(std, into, offset, nt):
                link(dve.reciprocal(std, std))
                tiles = nt // P
                cell_at = bass.AP(std.tensor, std.offset, [list(std.ap[0]), [1, tiles], [0, P]])
                return dve.tensor_tensor(view(into, offset, [P, tiles], [1, P]),
                                         view(ident, 0, [0, tiles], [1, P]), cell_at, ALU.mult)

            def clear_sum(n):
                dve.memset(sq_sum[:, 0:norm_tok(n)], 0.0).then_inc(s_sqs, 1)

            def add_squares(n, i, d):
                nt = norm_tok(n)
                at4 = (lambda x: i * 4 + x) if i is not None else (lambda x: x)
                dve.wait_ge(s_sq, at4(ND * n + d + 1))
                dve.wait_ge(s_sqs, at4((ND + 1) * n + d + 1))
                dve.tensor_tensor(sq_sum[:, 0:nt], sq_sum[:, 0:nt], sq[:, d % 2, 0:nt], ALU.add).then_inc(s_sqs, 1)

            def norm(n, to_u=True):
                nt = norm_tok(n)
                dve.wait_ge(s_std, n + 1)
                spread(r_cols[:, 0, 0:nt // P], diag, 0, nt).then_inc(s_diag, 1)
                if n == 0:
                    dve.wait_ge(s_cols, 1)
                    link(dve.tensor_copy(mod[:, :, 0:START], view(bank[6], 0, [1, 2], [2, START])))
                    norm_columns(0, 0, 0)
                    for j in range(AHEAD - 1):
                        split_lo(START, None, j)
                dve.wait_ge(s_bc, n + 1)
                if not to_u:
                    for d in range(ND):
                        dve.scalar_tensor_tensor(out=sig_a[:, d, 0:nt], in0=h[:, d, 0:nt],
                                                 scalar=cols[:, C_FIN + d:C_FIN + d + 1], in1=bank[5][:, 0:nt],
                                                 op0=ALU.mult, op1=ALU.mult).then_inc(s_fin, 1)
                    return

                def scaled(d):
                    for s in streams(nt):
                        dve.scalar_tensor_tensor(out=norm_t[:, d % 4, span(s)], in0=h[:, d, span(s)],
                                                       scalar=scale_c[:, s, d:d + 1], in1=bank[5][:, span(s)],
                                                       op0=ALU.mult, op1=ALU.mult).then_inc(s_nt, 2 * TOK // nt)

                def low(d):
                    dve.wait_ge(s_uhi, u_count(n) + d + 1)
                    for s in streams(nt):
                        ins = dve.scalar_tensor_tensor(out=u_lo[:, d, span(s)], in0=norm_t[:, d % 4, span(s)],
                                                       scalar=shift_c[:, s, d:d + 1],
                                                       in1=u_hi[:, d, span(s)].bitcast(F32),
                                                       op0=ALU.add, op1=ALU.subtract)
                    ins.then_inc(s_ulo, 1)

                for d in range(ND):
                    scaled(d)
                    if d:
                        low(d - 1)
                low(ND - 1)

            def residual(d, ps, nt):
                for s in streams(nt):
                    hd = h[:, bass.ds(d, 1), span(s)].rearrange("p a n -> p (a n)")
                    ins = dve.scalar_tensor_tensor(
                        out=hd, in0=ps[:, span(s)],
                        scalar=gate_c[:, s, bass.ds(d, 1)], in1=hd, op0=ALU.mult, op1=ALU.add)
                ins.then_inc(s_res, 1)

            def ffn(layer, which, n_norm):
                nt = ffn_tok(layer, which)
                k0 = 6 * which
                norm(n_norm)
                if n_norm == 0:
                    split_lo(START, None, AHEAD - 1)
                    dve.wait_ge(s_silu_c, 3)
                    dve.wait_ge(s_mland, 16)
                    link(dve.tensor_copy(masks[:], masks_f[:]))
                base = ffn_base(layer, which)
                hid = hid_count(layer, which)
                last_ffn = layer == NLAYER - 1 and which == 1
                ada_at = ADA.get((layer, f"ffn{which}"), (None, 0))[0]
                for part, n in enumerate(PARTS):
                    with dve.Fori(0, n // 2) as i:
                        for b in range(2):
                            split_lo(base, i, 2 * b + AHEAD)
                            dve.wait_ge(s_silu, i * 2 + (hid + b + 1))
                            dve.tensor_tensor(hid_t[:, b, 0:nt], silu_t[:, b, 0:nt], bank[2 * b + 1][:, 0:nt],
                                              ALU.mult).then_inc(s_up_free, 1)
                            dve.wait_ge(s_hid_hi, i * 2 + (hid + b + 1))
                            f = i * 2 + b
                            dve.tensor_tensor(
                                hid_lo[:, bass.ds(f, 1), 0:nt].rearrange("p a n -> p (a n)"), hid_t[:, b, 0:nt],
                                hid_hi[:, bass.ds(f, 1), 0:nt].rearrange("p a n -> p (a n)").bitcast(F32),
                                ALU.subtract).then_inc(s_hid_lo, 1)
                            split_lo(base, i, 2 * b + AHEAD + 1)
                        if ada_at is not None:
                            ada_pair(i, ada_at)
                    base += 2 * n
                    hid += n
                    if ada_at is not None:
                        ada_at += n
                    if part == 0:
                        gate_columns(layer, k0 + 2, 0.5)
                    rounds = ND // 4
                    final = last_ffn and part == len(PARTS) - 1
                    if final:
                        rounds -= 1
                    to_norm = part == len(PARTS) - 1
                    if to_norm:
                        if which == 0:
                            norm_columns(layer, 3, 1)
                        elif layer < NLAYER - 1:
                            norm_columns(layer + 1, 0, 0)
                        clear_sum(n_norm + 1)
                    with dve.Fori(0, rounds) as i:
                        for j in range(4):
                            dve.wait_ge(s_used, i * 4 + (base + j + 1))
                            residual(i * 4 + j, bank[4 + j], nt)
                            split_lo(base, i, j + AHEAD)
                            if to_norm:
                                add_squares(n_norm + 1, i, j)
                            elif ada_at is not None and j % 2:
                                ada_pair(i * 2 + j // 2, ada_at)
                    if final:
                        for j in range(4):
                            dve.wait_ge(s_used, base + 4 * rounds + j + 1)
                            residual(4 * rounds + j, bank[4 + j], nt)
                            if j == 0:
                                split_lo(base + 4 * rounds, None, AHEAD)
                            add_squares(n_norm + 1, None, 4 * rounds + j)
                    base += ND
                    if ada_at is not None:
                        ada_at += ND

            def prepare_head(layer, head):
                par = head % 2
                n = layer * NH + head
                lb_of = lambda d: lb[:, d, layer, head:head + 1]
                one_of = lambda d: one_lb[:, d, layer, head:head + 1]
                dve.wait_ge(s_proj, 6 * n + 5)
                for d in range(2):
                    dve.tensor_scalar(T[par][:, d, :], T[par][:, d, :], one_of(d), lb_of(d), ALU.mult, ALU.add)
                    key = S[par][:, 3 * d, :]
                    ins = dve.tensor_scalar(key, key, one_of(d), None, ALU.mult)
                link(ins)
                nt = ffn_tok(layer, 1)
                dve.tensor_tensor(S[par][:, 2, 0:nt], S[par][:, 0, 0:nt], S[par][:, 3, 0:nt], ALU.add
                                  ).then_inc(s_prep, 1)

            def prepare_step(n, step):
                Sh, Th = S[n % 2], T[n % 2]
                nt = ffn_tok(n // NH, 1)
                if step == 1:
                    link(dve.tensor_tensor(Sh[:, 2, 0:nt], Sh[:, 1, 0:nt], Th[:, 0, 0:nt], ALU.mult))
                    dve.tensor_tensor(Sh[:, 1, 0:nt], Sh[:, 1, 0:nt], Th[:, 1, 0:nt], ALU.mult).then_inc(s_prep, 1)
                    return
                hb = 1 << (step - 2)
                nb = ALL // (2 * hb)

                def carry(array, arrays, side, tokens, d):
                    at0 = array * ALL + side * hb
                    cut = [ALL, arrays], [2 * hb, tokens // (2 * hb)]
                    t = view(Sh, at0, *cut, [1, hb])
                    return dve.tensor_tensor(t, t, view(Th, d * ALL + (1 - side) * hb, *cut, [0, hb]), ALU.mult)

                if nt == ALL:
                    carry(0, 2, 0, ALL, 0)
                else:
                    carry(0, 1, 0, ALL, 0)
                    carry(1, 1, 0, nt, 1)
                if nt == ALL:
                    ins = carry(2, 2, 1, ALL, 0)
                else:
                    carry(2, 1, 1, nt, 0)
                    ins = carry(3, 1, 1, ALL, 1)
                ins.then_inc(s_prep, 1)

            def double_totals(n, step):
                hb = 1 << (step - 2)
                dve.wait_ge(s_prep, NSTEP * n + step + 1)
                both = lambda side: view(T[n % 2], side * hb, [ALL, 2], [2 * hb, ALL // (2 * hb)])
                link(dve.tensor_tensor(both(0), both(0), both(1), ALU.mult))

            def head_diag(n, nt):
                dve.wait_ge(s_hstd, n + 1)
                spread(r_cols[:, 1, 0:nt // P], head_t, 0, nt).then_inc(s_hdg, 1)

            def head_gate(n, nt):
                dve.wait_ge(s_hbc, n + 1)
                dve.tensor_tensor(head_t[:, 1, 0:nt], head_t[:, 1, 0:nt], bank[6][:, 0:nt], ALU.mult
                                  ).then_inc(s_at, 1)

            def head_lo(layer, head, nt):
                dve.wait_ge(s_ahi, layer * NH + head + 1)
                dve.tensor_tensor(a_lo[:, head, 0:nt], head_t[:, 1, 0:nt], a_hi[:, head, 0:nt].bitcast(F32),
                                  ALU.subtract).then_inc(s_head, 1)

            def merge(layer, head, step):
                par = head % 2
                ns = ffn_tok(layer, 1) // TOK
                dst = view(A[par], 0, [2 * TOK, ns], [TOK + P, 2], [1, P])
                src = view(bank[4 + step % 2], 0, [2 * P, ns], [P, 2], [1, P])
                if step == 0:
                    dve.tensor_tensor(dst, src, view(ident, 0, [0, ns], [0, 2], [1, P]), ALU.mult).then_inc(s_merge, 1)
                else:
                    dve.copy_predicated(dst, view(masks, (step - 1) * P, [0, ns], [0, 2], [1, P]), src
                                        ).then_inc(s_merge, 1)

            def mixer(layer, n_norm):
                nt = ffn_tok(layer, 1)
                base = mix_base(layer)
                n0 = layer * NH
                norm(n_norm)
                ada_at = ADA[(layer, "mix")][0]
                for j in range(8):
                    if j == 7:
                        prepare_head(layer, 0)
                    split_lo(base, None, j + AHEAD)
                    if j == 3 or (layer == 0 and j == 5):
                        ada_pair(0, ada_at)
                        ada_at += 2
                base += 8
                for head in range(NH):
                    n = n0 + head
                    par = head % 2
                    for piece in range(12):
                        j = piece // 2
                        lo_next = lambda: split_lo(base + j - (base + j) % 4, None, (base + j) % 4 + AHEAD)
                        if piece < NSTEP:
                            if 1 <= piece <= NLEVEL:
                                dve.wait_ge(s_mix, NLEVEL * n + piece)
                            else:
                                dve.wait_ge(s_score, NSTEP * n + piece + 1)
                            if piece < NSTEP - 1:
                                dve.wait_ge(s_prep, NSTEP * n + piece + 1)
                                if 1 <= piece <= NLEVEL + 1:
                                    dve.wait_ge(s_merge, (NLEVEL + 1) * n + piece)
                                prepare_step(n, piece + 1)
                            if piece % 2:
                                lo_next()
                            if piece <= NLEVEL:
                                dve.wait_ge(s_score, NSTEP * n + piece + 1)
                                merge(layer, head, piece)
                            if 1 <= piece <= NLEVEL:
                                double_totals(n, piece + 1)
                            if head and piece == 0:
                                head_diag(n - 1, nt)
                            if head and piece == 2:
                                head_gate(n - 1, nt)
                            if head and piece == 3:
                                head_lo(layer, head - 1, nt)
                        elif piece == NSTEP:
                            if head < NH - 1:
                                prepare_head(layer, head + 1)
                        else:
                            lo_next()
                            dve.wait_ge(s_av, n + 1)
                            dve.wait_ge(s_proj, 6 * (n + 1))
                            dve.wait_ge(s_hsq, n + 1)
                            hgw = cols[:, C_HGW + layer * NH + head:C_HGW + layer * NH + head + 1]
                            dve.scalar_tensor_tensor(out=head_t[:, 1, 0:nt], in0=bank[7][:, 0:nt], scalar=hgw,
                                                     in1=gs[:, par, 0:nt], op0=ALU.mult, op1=ALU.mult
                                                     ).then_inc(s_x1, 1)
                    base += 6
                dve.wait_ge(s_used, base)
                for t in range(nt // P // 2, nt // P):
                    ins = dve.tensor_copy(pv[:, t, :], bank[t][:])
                ins.then_inc(s_pvo, 1)
                head_diag(n0 + NH - 1, nt)
                head_gate(n0 + NH - 1, nt)
                head_lo(layer, NH - 1, nt)
                psc = lambda g: cols[:, C_PSC + layer * NG + g:C_PSC + layer * NG + g + 1]
                for g in range(NG):
                    dve.wait_ge(s_phi, layer * NG + g + 1)
                    dve.scalar_tensor_tensor(out=p_lo[:, g, 0:nt], in0=bank[4 + g][:, 0:nt], scalar=psc(g),
                                             in1=p_hi[:, g, 0:nt].bitcast(F32), op0=ALU.mult, op1=ALU.subtract
                                             ).then_inc(s_plo, 1)

                def merged_lo(d):
                    dve.wait_ge(s_uhi, d + (u_count(n_norm) + ND + 1))
                    dve.tensor_tensor(
                        m_lo[:, bass.ds(d, 1), 0:nt].rearrange("p a n -> p (a n)"),
                        sig_a[:, bass.ds(d, 1), 0:nt].rearrange("p a n -> p (a n)"),
                        m_hi[:, bass.ds(d, 1), 0:nt].rearrange("p a n -> p (a n)").bitcast(F32),
                        ALU.subtract).then_inc(s_ulo, 1)

                def merge_branches(i, b, before):
                    split_lo(base, i, 2 * b + AHEAD)
                    if before is not None:
                        merged_lo(before)
                    dve.wait_ge(s_used, i * 4 + (base + 2 * b + 2))
                    sa = sig_a[:, bass.ds(i * 2 + b, 1), 0:nt].rearrange("p a n -> p (a n)")
                    dve.tensor_tensor(mix_t[:, b, 0, 0:nt], sa, bank[4 * b + 1][:, 0:nt], ALU.mult)
                    dve.wait_ge(s_sgb, i * 2 + (layer * ND + b + 1))
                    dve.tensor_tensor(mix_t[:, b, 1, 0:nt], sig_b[:, b, 0:nt], bank[4 * b + 2][:, 0:nt],
                                      ALU.mult).then_inc(s_mt, 1)
                    dve.wait_ge(s_mt, i * 2 + (layer * ND + b + 1))
                    dve.tensor_tensor(sa, mix_t[:, b, 0, 0:nt], mix_t[:, b, 1, 0:nt], ALU.add).then_inc(s_mg, 1)
                    split_lo(base, i, 2 * b + AHEAD + 1)
                    if b == 0 and layer == 0:
                        ada_pair(i, ada_at)

                merge_branches(0, 0, None)
                merge_branches(0, 1, 0)
                with dve.Fori(1, ND // 2) as i:
                    merge_branches(i, 0, i * 2 - 1)
                    merge_branches(i, 1, i * 2)
                merged_lo(ND - 1)
                base += 2 * ND
                gate_columns(layer, 5, 1.0)
                norm_columns(layer, 6, 2)
                clear_sum(n_norm + 1)
                with dve.Fori(0, ND // 4) as i:
                    for j in range(4):
                        dve.wait_ge(s_used, i * 4 + (base + j + 1))
                        residual(i * 4 + j, bank[OUT_BANK[j]], nt)
                        split_lo(base, i, j + AHEAD)
                        add_squares(n_norm + 1, i, j)

            dve.memset(scale_c[:], 0.0).then_inc(s_up_free, 2)
            dve.memset(shift_c[:], 0.0).then_inc(s_res, 4)
            dve.memset(gate_c[:], 0.0).then_inc(s_mg, 2)
            dve.memset(lb[:], 0.0).then_inc(s_ada, 2)
            dve.wait_ge(s_load, 32)
            low = lambda l: view(cols, C_LB + l * NH, [NLAYER * NH, 2], [1, NH])
            cell = lambda t, l: view(lb_e, t * NLAYER * 2 * NH + l * NH, [NLAYER * NH, 2], [1, NH])
            one = lambda t: view(lb_e, t * NLAYER * 2 * NH, [NH, 2], [1, NH])
            link(dve.tensor_tensor(one(2), low(0), low(1), ALU.max))
            for l in range(NLAYER):
                link(dve.tensor_tensor(cell(0, l), low(l), one(2), ALU.subtract))
            dve.wait_ge(s_silu_c, 2)
            link(dve.tensor_tensor(one(3), cell(1, 0), cell(1, 1), ALU.add))
            link(dve.reciprocal(one(3), one(3)))
            for l in range(NLAYER):
                link(dve.tensor_tensor(cell(0, l), cell(1, l), one(3), ALU.mult))
            link(dve.tensor_tensor(lb[:, :, 0, :], cell(0, 0), cell(0, 0), ALU.subtract))
            link(dve.tensor_tensor(lb[:, :, 1, :], cell(0, 0), cell(0, 1), ALU.add))
            link(dve.tensor_tensor(lb[:, :, 1, :], lb[:, :, 1, :], cell(0, 0), ALU.subtract))
            link(dve.tensor_scalar(one_lb[:], lb[:], -1.0, 1.0, ALU.mult, ALU.add))
            clear_sum(0)
            for d in range(ND):
                add_squares(0, None, d)
            for b in range(4):
                dve.wait_ge(s_used, START - 1 + b // 2)
                dve.tensor_copy(start_rows[0:2, b, :], bank[b][0:2, :]).then_inc(s_rows, 1)
            n_norm = 0
            for layer in range(NLAYER):
                ffn(layer, 0, n_norm)
                mixer(layer, n_norm + 1)
                ffn(layer, 1, n_norm + 2)
                n_norm += 3
            norm(n_norm, to_u=False)


def ffn_tok(layer, which):
    return TOK if layer == NLAYER - 1 and which == 1 else ALL


def hid_count(layer, which):
    return (2 * layer + which) * NF


def res_count(layer, which):
    return layer * (2 * len(PARTS) + 1) * ND + which * (len(PARTS) + 1) * ND


def norm_res(n):
    return res_count(n // 3, 0) + (0, len(PARTS) * ND, (len(PARTS) + 1) * ND)[n % 3]


def norm_tok(n):
    return ALL if n < 3 * NLAYER - 1 else TOK


def u_count(n):
    return ND * (n + n // 3 + (n % 3 == 2))


def kernel(x, c, ctx, c_ctx, ada_w, ada_b, norm_w, ffn_wg, ffn_wu, ffn_wd, w_in, lower_bounds,
           hg_norm_w, pool_w, pool_scale, w_branch_a, w_branch_b, w_out, final_norm_w):
    import concourse.bacc as bacc
    from concourse.bass_utils import run_bass_kernel_spmd

    f = lambda a: np.asarray(a)
    x, c, ctx, c_ctx, ada_w, ada_b, norm_w = map(f, (x, c, ctx, c_ctx, ada_w, ada_b, norm_w))
    wg, wu, wd, w_in, lower_bounds = map(f, (ffn_wg, ffn_wu, ffn_wd, w_in, lower_bounds))
    hg_norm_w, pool_w, pool_scale, wa, wb = map(f, (hg_norm_w, pool_w, pool_scale, w_branch_a, w_branch_b))
    w_out, final_norm_w = f(w_out), f(final_norm_w)

    def columns(w):
        return w.reshape(ND, P, -1, P).transpose(2, 1, 0, 3).reshape(-1, P, UNIT)

    def wide(w):
        return w.reshape(4, 2, P, 512).transpose(0, 2, 1, 3).reshape(4, P, UNIT)

    def ffn_units(l, n):
        units, f0 = [], 0
        gate, up = columns(wg[l, n]), columns(wu[l, n])
        for size in PARTS:
            units.append(np.stack([gate[f0:f0 + size], up[f0:f0 + size]], 1).reshape(2 * size, P, UNIT))
            down = np.zeros((ND, P, 8, P), np.float32)
            down[:, :, :size] = wd[l, n][f0 * P:(f0 + size) * P].reshape(size, P, ND, P).transpose(2, 1, 0, 3)
            units.append(down.reshape(ND, P, UNIT))
            f0 += size
        return units

    def mixer_units(l):
        w = w_in[l]
        wq, wzf, wzb, wi, wgt, wpv = (w[:, 512 * n:512 * (n + 1)] for n in range(6))
        wga, wgb = columns(w[:, 3072:4096]), columns(w[:, 4096:5120])
        heads = np.stack([columns(m) for m in (wq, wzf, wzb, wgt)], 1)
        units = [wide(wi), heads[0]]
        for n in range(NH - 1):
            units += [heads[n + 1], wga[2 * n:2 * n + 2]]
        units += [wga[6:8], wide(wpv)]
        branch = np.stack([m.reshape(4, P, ND, P).transpose(2, 1, 0, 3) for m in (wa[l], wb[l])], 2)
        units.append(np.stack([wgb, branch.reshape(ND, P, UNIT)], 1).reshape(2 * ND, P, UNIT))
        units.append(columns(w_out[l]))
        return units

    start = ada_w[0][:, :START * P].reshape(ND, P, 2, UNIT).transpose(0, 2, 1, 3).reshape(START, P, UNIT)
    weights = np.concatenate([start] + [u for l in range(NLAYER) for u in ffn_units(l, 0) + mixer_units(l) + ffn_units(l, 1)])
    assert weights.shape == (N_UNITS, P, UNIT)
    adaw = np.ascontiguousarray(ada_w.transpose(0, 2, 1)).reshape(-1, P, D)[START:]
    resid = np.concatenate([x[0], ctx[0]]).T.reshape(ND, P, ALL).transpose(1, 0, 2)
    cols = np.concatenate([norm_w.reshape(-1, P), ada_b.reshape(-1, P), hg_norm_w.reshape(-1, P),
                           pool_scale.reshape(-1, P), lower_bounds.reshape(-1, P), final_norm_w.reshape(-1, P)]).T
    assert cols.shape == (P, N_COLS)

    def box_1d(n, w):
        m = np.zeros((n, n), np.float64)
        for i in range(n):
            lo, hi = max(i - w // 2, 0), min(i + w - w // 2, n)
            m[i, lo:hi] = 1.0 / (hi - lo)
        return m

    box = np.zeros((2, P, 2, NG, TOK), np.float32)
    for g, w in enumerate(WINDOWS):
        grid = np.kron(box_1d(TOK // GRID_W, w), box_1d(GRID_W, w))
        for s, m in enumerate((grid, box_1d(TOK, w))):
            box[s, :, :, g, :] = (m - np.eye(TOK)).T.reshape(2, P, TOK).transpose(1, 0, 2)
    i = np.arange(P)
    masks = np.stack([((i[:, None] >> (n + 1)) == (i[None] >> (n + 1))) & ((i[:, None] >> n) != (i[None] >> n))
                      for n in range(NLEVEL)], 1).astype(np.float32)

    arrays = {
        "resid": resid, "c": np.stack([c[0], c_ctx]),
        "c_cols": np.stack([c[0], c_ctx]).reshape(2, ND, P).transpose(2, 1, 0), "cols": cols,
        "poolw": pool_w.transpose(0, 2, 1, 3), "box": box, "masks": masks,
        "ident": np.eye(P, dtype=np.float32), "weights": weights, "adaw": adaw,
    }
    nc = bacc.Bacc("TRN2", target_bir_lowering=False, num_devices=1)
    args = []
    for name, a in arrays.items():
        arrays[name] = a = np.ascontiguousarray(a)
        args.append(nc.dram_tensor(name, a.shape, mybir.dt.from_np(a.dtype), kind="ExternalInput").ap())
    out = nc.dram_tensor("out", (P, ND, TOK), F32, kind="ExternalOutput").ap()
    program(nc, *args, out)
    got = run_bass_kernel_spmd(nc, [arrays], core_ids=[0]).results[0]["out"]
    return np.ascontiguousarray(got.transpose(2, 1, 0).reshape(1, TOK, D))
```
